# Optimizing a Trainium2 kernel written in Bass

```python
import jax, jax.numpy as jnp
from jax import lax
import numpy as np

D_MODEL = 1024
BATCH = 1
SEQ = 256
DEPTH = 2

HEAD_DIM = 64
NSA_HEADS = 8
NSA_KV_GROUPS = 2
NSA_HPG = NSA_HEADS // NSA_KV_GROUPS
CMP_LEN = 32
CMP_STRIDE = 16
CMP_HIDDEN = 256
SEL_BLOCK = 64
SEL_TOPK = 16
WINDOW = 512
NSA_QBLOCK = 64
FORCE_BONUS = 1e4
GLA_HEADS = 4
GLA_DK = 32
GLA_DV = 64
GLA_RANK = 16
GLA_TAU = 16.0
GLA_CHUNK = 64
SG_GROUPS = 4
SG_CH = 64
SG_CHUNK = 128
NSA_W = NSA_HEADS * HEAD_DIM
GLA_W = GLA_HEADS * GLA_DV
SG_W = SG_GROUPS * SG_CH
D_MIX = NSA_W + GLA_W + SG_W
KV_W = NSA_KV_GROUPS * HEAD_DIM
IN_SIZES = (NSA_W, KV_W, KV_W, KV_W, KV_W, KV_W, KV_W, NSA_HEADS * 3,
            GLA_HEADS * GLA_DK, GLA_HEADS * GLA_DK, GLA_W, GLA_RANK, GLA_W, 2 * SG_W)
D_IN = sum(IN_SIZES)
D_FF = -(-8 * D_MODEL // (3 * 256)) * 256
ROPE_THETA = 10000.0
NORM_EPS = 1e-6


def rmsnorm(x, g):
    xf = x.astype(jnp.float32)
    y = xf * lax.rsqrt(jnp.mean(xf * xf, axis=-1, keepdims=True) + NORM_EPS)
    return (y * g.astype(jnp.float32)).astype(x.dtype)

def layernorm(x, g, b):
    xf = x.astype(jnp.float32)
    mu = jnp.mean(xf, axis=-1, keepdims=True)
    var = jnp.mean(jnp.square(xf - mu), axis=-1, keepdims=True)
    y = (xf - mu) * lax.rsqrt(var + NORM_EPS)
    return (y * g.astype(jnp.float32) + b.astype(jnp.float32)).astype(x.dtype)

def rope(x, pos):
    half = x.shape[-1] // 2
    inv = 1.0 / (ROPE_THETA ** (jnp.arange(half, dtype=jnp.float32) / half))
    ang = pos[:, None] * inv[None, :]
    cos = jnp.cos(ang)[None, :, None, :]
    sin = jnp.sin(ang)[None, :, None, :]
    xf = x.astype(jnp.float32)
    x1, x2 = xf[..., :half], xf[..., half:]
    return jnp.concatenate([x1 * cos - x2 * sin, x2 * cos + x1 * sin], axis=-1).astype(x.dtype)

def masked_softmax(s, mask):
    s = jnp.where(mask, s.astype(jnp.float32), -jnp.inf)
    m = jnp.max(s, axis=-1, keepdims=True)
    m = jnp.where(jnp.isfinite(m), m, 0.0)
    e = jnp.exp(s - m)
    d = jnp.sum(e, axis=-1, keepdims=True)
    return e / jnp.where(d > 0, d, 1.0)

def compress_blocks(k_raw, pos_emb, w1, w2):
    B, S, G, hd = k_raw.shape
    nc = (S - CMP_LEN) // CMP_STRIDE + 1
    idx = np.arange(nc)[:, None] * CMP_STRIDE + np.arange(CMP_LEN)[None, :]
    blk = k_raw[:, idx] + pos_emb[None, None, :, None, :]
    blk = blk.transpose(0, 1, 3, 2, 4).reshape(B, nc, G, CMP_LEN * hd)
    return jax.nn.gelu(blk @ w1) @ w2

def importance_map(nc, nsb):
    cs = np.arange(nc) * CMP_STRIDE
    ce = cs + CMP_LEN
    bs = np.arange(nsb) * SEL_BLOCK
    be = bs + SEL_BLOCK
    ov = np.clip(np.minimum(ce[:, None], be[None, :]) - np.maximum(cs[:, None], bs[None, :]), 0, None)
    return jnp.asarray(ov / CMP_LEN, jnp.float32)

def nsa_mixer(q, k_cmp_raw, v_cmp_raw, k_slc, v_slc, k_win, v_win, gates,
              cmp_pos_k, cmp_w1_k, cmp_w2_k, cmp_pos_v, cmp_w1_v, cmp_w2_v):
    B, S, _ = q.shape
    G, HPG, hd, QB = NSA_KV_GROUPS, NSA_HPG, HEAD_DIM, NSA_QBLOCK
    pos = jnp.arange(S, dtype=jnp.float32)
    q = rope(q.reshape(B, S, NSA_HEADS, hd), pos).reshape(B, S, G, HPG, hd) * (hd ** -0.5)
    nc = (S - CMP_LEN) // CMP_STRIDE + 1
    cmp_end_np = np.arange(nc) * CMP_STRIDE + CMP_LEN - 1
    kc = compress_blocks(k_cmp_raw.reshape(B, S, G, hd), cmp_pos_k, cmp_w1_k, cmp_w2_k)
    kc = rope(kc, jnp.asarray(cmp_end_np, jnp.float32))
    vc = compress_blocks(v_cmp_raw.reshape(B, S, G, hd), cmp_pos_v, cmp_w1_v, cmp_w2_v)
    cmp_end = jnp.asarray(cmp_end_np, jnp.int32)
    nsb = S // SEL_BLOCK
    topk = min(SEL_TOPK, nsb)
    ks = rope(k_slc.reshape(B, S, G, hd), pos)
    kb = ks.reshape(B, nsb, SEL_BLOCK, G, hd).transpose(0, 3, 1, 2, 4)
    vb = v_slc.reshape(B, nsb, SEL_BLOCK, G, hd).transpose(0, 3, 1, 2, 4)
    imp_map = importance_map(nc, nsb)
    blk_id = jnp.arange(nsb)
    bi = jnp.arange(B)[:, None, None, None]
    gi = jnp.arange(G)[None, :, None, None]
    kw = jnp.pad(rope(k_win.reshape(B, S, G, hd), pos), ((0, 0), (WINDOW, 0), (0, 0), (0, 0)))
    vw = jnp.pad(v_win.reshape(B, S, G, hd), ((0, 0), (WINDOW, 0), (0, 0), (0, 0)))
    gates = jax.nn.sigmoid(gates).reshape(B, S, G, HPG, 3)

    def query_block(i):
        s0 = i * QB
        t = s0 + jnp.arange(QB)
        qb = lax.dynamic_slice_in_dim(q, s0, QB, axis=1)
        gb = lax.dynamic_slice_in_dim(gates, s0, QB, axis=1)
        s = jnp.einsum('bqghd,bcgd->bghqc', qb, kc)
        p_cmp = masked_softmax(s, (cmp_end[None, :] <= t[:, None])[None, None, None])
        o_cmp = jnp.einsum('bghqc,bcgd->bqghd', p_cmp.astype(vc.dtype), vc)
        imp = jnp.einsum('bghqc,cn->bgqn', p_cmp, imp_map)
        tb = t // SEL_BLOCK
        valid = blk_id[None, :] * SEL_BLOCK <= t[:, None]
        forced = (blk_id[None, :] == 0) | (blk_id[None, :] == tb[:, None]) | (blk_id[None, :] == tb[:, None] - 1)
        score = jnp.where(valid, imp + jnp.where(forced, FORCE_BONUS, 0.0), -jnp.inf)
        _, idx = lax.top_k(score, topk)
        ksel = kb[bi, gi, idx].reshape(B, G, QB, topk * SEL_BLOCK, hd)
        vsel = vb[bi, gi, idx].reshape(B, G, QB, topk * SEL_BLOCK, hd)
        tok = (idx[..., None] * SEL_BLOCK + jnp.arange(SEL_BLOCK)).reshape(B, G, 1, QB, topk * SEL_BLOCK)
        s = jnp.einsum('bqghd,bgqmd->bghqm', qb, ksel)
        p = masked_softmax(s, tok <= t[None, None, None, :, None])
        o_slc = jnp.einsum('bghqm,bgqmd->bqghd', p.astype(vsel.dtype), vsel)
        kwb = lax.dynamic_slice_in_dim(kw, s0, WINDOW + QB, axis=1)
        vwb = lax.dynamic_slice_in_dim(vw, s0, WINDOW + QB, axis=1)
        kpos = s0 - WINDOW + jnp.arange(WINDOW + QB)
        wmask = (kpos[None, :] <= t[:, None]) & (kpos[None, :] > t[:, None] - WINDOW) & (kpos[None, :] >= 0)
        s = jnp.einsum('bqghd,bkgd->bghqk', qb, kwb)
        p = masked_softmax(s, wmask[None, None, None])
        o_win = jnp.einsum('bghqk,bkgd->bqghd', p.astype(vwb.dtype), vwb)
        return gb[..., 0:1] * o_cmp + gb[..., 1:2] * o_slc + gb[..., 2:3] * o_win

    out = lax.map(query_block, jnp.arange(S // QB))
    return out.transpose(1, 0, 2, 3, 4, 5).reshape(B, S, NSA_W)

def gla_mixer(q, k, v, a_lr, r, w_up, b_up, norm_g):
    B, S, _ = q.shape
    H, DK, DV, C = GLA_HEADS, GLA_DK, GLA_DV, GLA_CHUNK
    f32 = jnp.float32
    q = q.reshape(B, S, H, DK).astype(f32) * (DK ** -0.5)
    k = k.reshape(B, S, H, DK).astype(f32)
    v = v.reshape(B, S, H, DV).astype(f32)
    g = jax.nn.log_sigmoid((a_lr @ w_up + b_up).astype(f32)).reshape(B, S, H, DK) / GLA_TAU
    n = S // C

    def to_chunks(a):
        return a.reshape(B, n, C, H, a.shape[-1]).transpose(1, 0, 3, 2, 4)

    causal = jnp.tril(jnp.ones((C, C), dtype=bool))

    def step(state, inp):
        qc, kc, vc, gc = inp
        bcum = jnp.cumsum(gc, axis=2)
        o_inter = jnp.einsum('bhck,bhkv->bhcv', qc * jnp.exp(bcum), state)
        diff = bcum[:, :, :, None, :] - bcum[:, :, None, :, :]
        decay = jnp.exp(jnp.where(causal[None, None, :, :, None], diff, -jnp.inf))
        attn = jnp.einsum('bhik,bhjk,bhijk->bhij', qc, kc, decay)
        o_intra = jnp.einsum('bhij,bhjv->bhiv', attn, vc)
        blast = bcum[:, :, -1:, :]
        state = jnp.exp(blast[:, :, 0, :])[..., None] * state + jnp.einsum(
            'bhjk,bhjv->bhkv', kc * jnp.exp(blast - bcum), vc)
        return state, o_inter + o_intra

    state0 = jnp.zeros((B, H, DK, DV), f32)
    _, o = lax.scan(step, state0, (to_chunks(q), to_chunks(k), to_chunks(v), to_chunks(g)))
    o = o.transpose(1, 0, 3, 2, 4).reshape(B, S, H, DV)
    o = rmsnorm(o, norm_g) * jax.nn.silu(r.astype(f32)).reshape(B, S, H, DV)
    return o.reshape(B, S, GLA_W).astype(r.dtype)

def spatial_gating(uv, ln_g, ln_b, w_s, b_s):
    B, S, _ = uv.shape
    nch = S // SG_CHUNK
    u, v = jnp.split(jax.nn.gelu(uv), 2, axis=-1)
    v = layernorm(v, ln_g, ln_b).reshape(B, nch, SG_CHUNK, SG_GROUPS, SG_CH)
    w = jnp.tril(w_s)
    s = jnp.einsum('gij,bnjgc->bnigc', w, v) + b_s.T[None, None, :, :, None]
    out = u.reshape(B, nch, SG_CHUNK, SG_GROUPS, SG_CH) * s
    return out.reshape(B, S, SG_W)

def split_columns(z):
    offs = np.cumsum(IN_SIZES)[:-1]
    return jnp.split(z, [int(o) for o in offs], axis=-1)

def first_inputs(seed: int = 0) -> dict:
    key = jax.random.key(seed)
    ks = jax.random.split(key, 32)
    L = DEPTH
    res = (2.0 * DEPTH) ** -0.5

    def nrm(k, shape, scale):
        return jax.random.normal(k, shape, jnp.float32) * scale

    def gain(k, shape):
        return 1.0 + nrm(k, shape, 0.02)

    return {
        "x": nrm(ks[0], (BATCH, SEQ, D_MODEL), 1.0),
        "attn_norm": gain(ks[1], (L, D_MODEL)),
        "w_in": nrm(ks[2], (L, D_MODEL, D_IN), D_MODEL ** -0.5),
        "cmp_pos_k": nrm(ks[3], (L, CMP_LEN, HEAD_DIM), 0.1),
        "cmp_w1_k": nrm(ks[4], (L, CMP_LEN * HEAD_DIM, CMP_HIDDEN), (CMP_LEN * HEAD_DIM) ** -0.5),
        "cmp_w2_k": nrm(ks[5], (L, CMP_HIDDEN, HEAD_DIM), CMP_HIDDEN ** -0.5),
        "cmp_pos_v": nrm(ks[6], (L, CMP_LEN, HEAD_DIM), 0.1),
        "cmp_w1_v": nrm(ks[7], (L, CMP_LEN * HEAD_DIM, CMP_HIDDEN), (CMP_LEN * HEAD_DIM) ** -0.5),
        "cmp_w2_v": nrm(ks[8], (L, CMP_HIDDEN, HEAD_DIM), CMP_HIDDEN ** -0.5),
        "gla_w_up": nrm(ks[9], (L, GLA_RANK, GLA_HEADS * GLA_DK), GLA_RANK ** -0.5),
        "gla_b_up": nrm(ks[10], (L, GLA_HEADS * GLA_DK), 0.1),
        "gla_norm": gain(ks[11], (L, GLA_DV)),
        "sg_ln_g": gain(ks[12], (L, SG_W)),
        "sg_ln_b": nrm(ks[13], (L, SG_W), 0.02),
        "sg_w": nrm(ks[14], (L, SG_GROUPS, SG_CHUNK, SG_CHUNK), SG_CHUNK ** -0.5),
        "sg_b": 1.0 + nrm(ks[15], (L, SG_GROUPS, SG_CHUNK), 0.1),
        "w_out": nrm(ks[16], (L, D_MIX, D_MODEL), D_MIX ** -0.5 * res),
        "ffn_norm": gain(ks[17], (L, D_MODEL)),
        "w_gate": nrm(ks[18], (L, D_MODEL, D_FF), D_MODEL ** -0.5),
        "w_up": nrm(ks[19], (L, D_MODEL, D_FF), D_MODEL ** -0.5),
        "w_down": nrm(ks[20], (L, D_FF, D_MODEL), D_FF ** -0.5 * res),
        "final_norm": gain(ks[21], (D_MODEL,)),
    }

def first_block(x, attn_norm, w_in, cmp_pos_k, cmp_w1_k, cmp_w2_k, cmp_pos_v, cmp_w1_v, cmp_w2_v,
              gla_w_up, gla_b_up, gla_norm, sg_ln_g, sg_ln_b, sg_w, sg_b, w_out,
              ffn_norm, w_gate, w_up, w_down, final_norm):
    for l in range(DEPTH):
        h = rmsnorm(x, attn_norm[l])
        (q, kc, vc, ksl, vsl, kwn, vwn, gts, gq, gk, gv, ga, gr, uv) = split_columns(h @ w_in[l])
        o_nsa = nsa_mixer(q, kc, vc, ksl, vsl, kwn, vwn, gts,
                          cmp_pos_k[l], cmp_w1_k[l], cmp_w2_k[l], cmp_pos_v[l], cmp_w1_v[l], cmp_w2_v[l])
        o_gla = gla_mixer(gq, gk, gv, ga, gr, gla_w_up[l], gla_b_up[l], gla_norm[l])
        o_sg = spatial_gating(uv, sg_ln_g[l], sg_ln_b[l], sg_w[l], sg_b[l])
        x = x + jnp.concatenate([o_nsa, o_gla.astype(x.dtype), o_sg], axis=-1) @ w_out[l]
        h = rmsnorm(x, ffn_norm[l])
        x = x + (jax.nn.silu(h @ w_gate[l]) * (h @ w_up[l])) @ w_down[l]
    return rmsnorm(x, final_norm)


DEPTH_2 = 1

BLOCK = 128
DIL_PATTERNS = ((128, 1), (512, 4), (2048, 16))
N_DIL_GROUPS = 3
DIL_HEADS_PER_GROUP = 8
DIL_HEADS = N_DIL_GROUPS * DIL_HEADS_PER_GROUP
DIL_WIDTH = DIL_HEADS * HEAD_DIM
DIL_MERGED = DIL_HEADS_PER_GROUP * HEAD_DIM
SWA_WINDOW = 128
SWA_Q_HEADS = 16
SWA_KV_HEADS = 2
SWA_Q_WIDTH = SWA_Q_HEADS * HEAD_DIM
SWA_KV_WIDTH = SWA_KV_HEADS * HEAD_DIM
IN_WIDTHS = (DIL_WIDTH, DIL_WIDTH, DIL_WIDTH, SWA_Q_WIDTH, SWA_KV_WIDTH, SWA_KV_WIDTH, D_MODEL, D_MODEL)
IN_WIDTH = sum(IN_WIDTHS)
MOE_GROUPS = 4
EXPERTS_PER_GROUP = 8
N_EXPERTS = MOE_GROUPS * EXPERTS_PER_GROUP
TOP_K = 2
D_EXPERT = 512
RMS_EPS = 1e-6


def rmsnorm_2(x, gain):
    x32 = x.astype(jnp.float32)
    y = x32 * lax.rsqrt(jnp.mean(x32 * x32, axis=-1, keepdims=True) + RMS_EPS)
    return (y * gain.astype(jnp.float32)).astype(x.dtype)

def alibi_slopes(n):
    return (2.0 ** (-8.0 * np.arange(1, n + 1) / n)).astype(np.float32)

def split_cols(proj, widths):
    offs = [0]
    for w in widths:
        offs.append(offs[-1] + w)
    return [proj[..., offs[i]:offs[i + 1]] for i in range(len(widths))]

def banded_attention(q, k, v, slopes, max_back, unit, sinks=None):
    b, s, l, hq, hd = q.shape
    hkv = k.shape[3]
    rep = hq // hkv
    nb = -(-l // BLOCK)
    lp = nb * BLOCK
    pad = [(0, 0), (0, 0), (0, lp - l), (0, 0), (0, 0)]
    qb = jnp.pad(q, pad).reshape(b, s, nb, BLOCK, hkv, rep, hd)
    kb = jnp.pad(k, pad).reshape(b, s, nb, BLOCK, hkv, hd)
    vb = jnp.pad(v, pad).reshape(b, s, nb, BLOCK, hkv, hd)

    def with_prev(z):
        prev = jnp.pad(z[:, :, :-1], [(0, 0), (0, 0), (1, 0), (0, 0), (0, 0), (0, 0)])
        return jnp.concatenate([prev, z], axis=3)

    kk, vv = with_prev(kb), with_prev(vb)
    scores = jnp.einsum('bsnqgrd,bsnkgd->bsngrqk', qb, kk,
                        preferred_element_type=jnp.float32) * (hd ** -0.5)
    a = np.arange(BLOCK)[:, None]
    c = np.arange(2 * BLOCK)[None, :]
    delta = a + BLOCK - c
    band = (delta >= 0) & (delta <= max_back)
    valid = band[None] & ((np.arange(nb)[:, None, None] > 0) | (c >= BLOCK)[None])
    bias = (-slopes.reshape(hkv, rep)[:, :, None, None] * (delta * unit)[None, None]).astype(np.float32)
    scores = jnp.where(valid[None, None, :, None, None], scores + bias, -jnp.inf)
    m = scores.max(axis=-1)
    if sinks is not None:
        sink = sinks.astype(jnp.float32).reshape(hkv, rep)[:, :, None]
        m = jnp.maximum(m, sink)
    p = jnp.exp(scores - m[..., None])
    denom = p.sum(axis=-1)
    if sinks is not None:
        denom = denom + jnp.exp(sink - m)
    out = jnp.einsum('bsngrqk,bsnkgd->bsnqgrd', p, vv.astype(jnp.float32))
    denom_t = jnp.moveaxis(denom, -1, 3)
    out = (out / denom_t[..., None]).reshape(b, s, lp, hq, hd)[:, :, :l]
    lse = (jnp.moveaxis(m, -1, 3) + jnp.log(denom_t)).reshape(b, s, lp, hq)[:, :, :l]
    return out.astype(q.dtype), lse

def dilated_attention(q, k, v):
    b, t = q.shape[:2]
    slopes = alibi_slopes(DIL_HEADS)
    outs, lses = [], []
    for gi, (window, dil) in enumerate(DIL_PATTERNS):
        lo, hi = gi * DIL_HEADS_PER_GROUP, (gi + 1) * DIL_HEADS_PER_GROUP
        l = t // dil

        def to_streams(z):
            return z[:, :, lo:hi].reshape(b, l, dil, DIL_HEADS_PER_GROUP, HEAD_DIM).transpose(0, 2, 1, 3, 4)

        o, lse = banded_attention(to_streams(q), to_streams(k), to_streams(v),
                                  slopes[lo:hi], window // dil, dil)
        outs.append(o.transpose(0, 2, 1, 3, 4).reshape(b, t, DIL_HEADS_PER_GROUP, HEAD_DIM))
        lses.append(lse.transpose(0, 2, 1, 3).reshape(b, t, DIL_HEADS_PER_GROUP))
    alpha = jax.nn.softmax(jnp.stack(lses, axis=2), axis=2)
    y = jnp.einsum('btgh,btghd->bthd', alpha.astype(q.dtype), jnp.stack(outs, axis=2))
    return y.reshape(b, t, DIL_MERGED)

def swa_sink_attention(q, k, v, sinks):
    b, t = q.shape[:2]
    out, _ = banded_attention(q[:, None], k[:, None], v[:, None], alibi_slopes(SWA_Q_HEADS),
                              SWA_WINDOW - 1, 1, sinks=sinks)
    return out[:, 0].reshape(b, t, SWA_Q_WIDTH)

def hier_moe(h, w_group, b_group, w_router, b_router, w_e_gate, w_e_up, w_e_down):
    b, t, d = h.shape
    hf = h.reshape(b * t, d)
    g_logits = (hf @ w_group).astype(jnp.float32) + b_group.astype(jnp.float32)
    g_probs = jax.nn.softmax(g_logits, axis=-1)
    g_top = jnp.argmax(g_logits, axis=-1)
    g_w = jnp.take_along_axis(g_probs, g_top[:, None], axis=1)
    e_logits = ((hf @ w_router).astype(jnp.float32) + b_router.astype(jnp.float32)).reshape(
        -1, MOE_GROUPS, EXPERTS_PER_GROUP)
    e_logits = jnp.take_along_axis(e_logits, g_top[:, None, None], axis=1)[:, 0]
    e_w, e_idx = lax.top_k(jax.nn.softmax(e_logits, axis=-1), TOP_K)
    e_w = e_w / e_w.sum(axis=-1, keepdims=True)
    ids = g_top[:, None] * EXPERTS_PER_GROUP + e_idx
    gates = jnp.einsum('nk,nke->ne', g_w * e_w, jax.nn.one_hot(ids, N_EXPERTS, dtype=jnp.float32))
    out = jnp.zeros_like(hf)
    for e in range(N_EXPERTS):
        a = jax.nn.silu(hf @ w_e_gate[e]) * (hf @ w_e_up[e])
        out = out + gates[:, e:e + 1].astype(hf.dtype) * (a @ w_e_down[e])
    return out.reshape(b, t, d)

def second_inputs(seed: int = 0) -> dict:
    key = jax.random.key(seed)
    ks = jax.random.split(key, 20)
    f32 = jnp.float32

    def nrm(k, shape, fan_in):
        return jax.random.normal(k, shape, f32) * (fan_in ** -0.5)

    return {
        'x': jax.random.normal(ks[0], (BATCH, SEQ, D_MODEL), f32),
        'g_mix': 1.0 + 0.05 * jax.random.normal(ks[1], (DEPTH_2, D_MODEL), f32),
        'w_in': nrm(ks[2], (DEPTH_2, D_MODEL, IN_WIDTH), D_MODEL),
        'sinks': jax.random.normal(ks[3], (DEPTH_2, SWA_Q_HEADS), f32),
        'w_br_dil': nrm(ks[4], (DEPTH_2, DIL_MERGED, D_MODEL), DIL_MERGED),
        'w_br_swa': nrm(ks[5], (DEPTH_2, SWA_Q_WIDTH, D_MODEL), SWA_Q_WIDTH),
        'w_out': nrm(ks[6], (DEPTH_2, D_MODEL, D_MODEL), D_MODEL),
        'g_ffn': 1.0 + 0.05 * jax.random.normal(ks[7], (DEPTH_2, D_MODEL), f32),
        'w_group': nrm(ks[8], (DEPTH_2, D_MODEL, MOE_GROUPS), D_MODEL),
        'b_group': 0.01 * jax.random.normal(ks[9], (DEPTH_2, MOE_GROUPS), f32),
        'w_router': nrm(ks[10], (DEPTH_2, D_MODEL, N_EXPERTS), D_MODEL),
        'b_router': 0.01 * jax.random.normal(ks[11], (DEPTH_2, N_EXPERTS), f32),
        'w_e_gate': nrm(ks[12], (DEPTH_2, N_EXPERTS, D_MODEL, D_EXPERT), D_MODEL),
        'w_e_up': nrm(ks[13], (DEPTH_2, N_EXPERTS, D_MODEL, D_EXPERT), D_MODEL),
        'w_e_down': nrm(ks[14], (DEPTH_2, N_EXPERTS, D_EXPERT, D_MODEL), D_EXPERT),
        'g_final': 1.0 + 0.05 * jax.random.normal(ks[15], (D_MODEL,), f32),
    }

def second_block(x, g_mix, w_in, sinks, w_br_dil, w_br_swa, w_out, g_ffn, w_group, b_group,
              w_router, b_router, w_e_gate, w_e_up, w_e_down, g_final):
    b, t, _ = x.shape
    for l in range(DEPTH_2):
        h = rmsnorm_2(x, g_mix[l])
        proj = h @ w_in[l]
        q_d, k_d, v_d, q_s, k_s, v_s, gate_d, gate_s = split_cols(proj, IN_WIDTHS)
        y_dil = dilated_attention(q_d.reshape(b, t, DIL_HEADS, HEAD_DIM),
                                  k_d.reshape(b, t, DIL_HEADS, HEAD_DIM),
                                  v_d.reshape(b, t, DIL_HEADS, HEAD_DIM))
        y_swa = swa_sink_attention(q_s.reshape(b, t, SWA_Q_HEADS, HEAD_DIM),
                                   k_s.reshape(b, t, SWA_KV_HEADS, HEAD_DIM),
                                   v_s.reshape(b, t, SWA_KV_HEADS, HEAD_DIM), sinks[l])
        mixed = (jax.nn.sigmoid(gate_d) * (y_dil @ w_br_dil[l])
                 + jax.nn.sigmoid(gate_s) * (y_swa @ w_br_swa[l]))
        x = x + mixed @ w_out[l]
        x = x + hier_moe(rmsnorm_2(x, g_ffn[l]), w_group[l], b_group[l], w_router[l], b_router[l],
                         w_e_gate[l], w_e_up[l], w_e_down[l])
    return rmsnorm_2(x, g_final)


def setup_inputs(seed=0):
    out = dict(first_inputs(seed))
    for name, value in second_inputs(seed + 1).items():
        if name != "x":
            out[name + "_2"] = value
    return out


def reference(
    x, attn_norm, w_in, cmp_pos_k, cmp_w1_k, cmp_w2_k, cmp_pos_v, cmp_w1_v, cmp_w2_v, gla_w_up,
    gla_b_up, gla_norm, sg_ln_g, sg_ln_b, sg_w, sg_b, w_out, ffn_norm, w_gate, w_up, w_down,
    final_norm, g_mix_2, w_in_2, sinks_2, w_br_dil_2, w_br_swa_2, w_out_2, g_ffn_2, w_group_2,
    b_group_2, w_router_2, b_router_2, w_e_gate_2, w_e_up_2, w_e_down_2, g_final_2,
):
    x = first_block(
        x, attn_norm, w_in, cmp_pos_k, cmp_w1_k, cmp_w2_k, cmp_pos_v, cmp_w1_v, cmp_w2_v,
        gla_w_up, gla_b_up, gla_norm, sg_ln_g, sg_ln_b, sg_w, sg_b, w_out, ffn_norm, w_gate,
        w_up, w_down, final_norm,
    )
    return second_block(
        x, g_mix_2, w_in_2, sinks_2, w_br_dil_2, w_br_swa_2, w_out_2, g_ffn_2, w_group_2,
        b_group_2, w_router_2, b_router_2, w_e_gate_2, w_e_up_2, w_e_down_2, g_final_2,
    )


_drawn_inputs = setup_inputs


def setup_inputs(seed=0):
    import zlib

    import numpy as np

    out = dict(_drawn_inputs(seed))
    spreads = {}
    factors = {'cmp_pos_k': 4.859,
     'gla_b_up': 2.996,
     'gla_norm': 4.083,
     'sg_ln_g': 3.592,
     'sg_ln_b': 5.397,
     'b_group_2': 4.279,
     'b_router_2': 3.219}
    for name, (base, spread) in spreads.items():
        noise = np.random.default_rng([zlib.crc32(name.encode()), seed]).standard_normal(out[name].shape)
        drawn = base * np.exp(spread * noise) if base else spread * noise
        out[name] = __import__('jax').numpy.asarray(drawn.astype(out[name].dtype))
    for name, factor in factors.items():
        out[name] = (out[name] * factor).astype(out[name].dtype)
    return out
```

```python
from contextlib import ExitStack

import numpy as np
import concourse.bass as bass
from concourse import mybir

F32 = mybir.dt.float32
F32R = mybir.dt.float32r
U8 = mybir.dt.uint8
I32 = mybir.dt.int32
ACT = mybir.ActivationFunctionType
ALU = mybir.AluOpType
AX = mybir.AxisListType.X

P = 128
SEQ = 256
TT = SEQ // P
D = 1024
KC = D // P
LAYERS = 2
PW = 2048
CW = PW // KC
SLOTS = 3
ARENA = 15960
EXPERT_R = 11648
EPS = 1e-6
NEG = -1e30
HD = 64
ROPE_THETA = 10000.0

HEADS, GROUPS = 8, 2
CMP_LEN, CMP_STRIDE, CMP_HIDDEN = 32, 16, 256
NCMP = (SEQ - CMP_LEN) // CMP_STRIDE + 1
CPAD = 32
LP = CMP_LEN // 2
DK, DV, GH = 32, 64, 4
TAU = 16.0
DFF = 2816
UNITS1 = DFF // CW
LEVELS = [64, 32, 16, 8, 4, 2, 1]
IN_SIZES = (512, 128, 128, 128, 128, 128, 128, 24, 128, 128, 256, 16, 256, 512)
Z_GQ, Z_GK, Z_GV, Z_GR, Z_U, Z_V, Z_Q, Z_SLC, Z_WIN, Z_KC, Z_VC = (
    0, 128, 256, 512, 768, 1024, 1280, 1792, 2048, 2304, 2432)
ZW = 2560
GATES, RANK = 24, 16

P_GQK, P_GV, P_GR, P_U, P_V, P_Q0, P_Q1, P_SLC, P_WIN, P_CMP = range(10)
P_CMPK, P_CMPV, P_OUT, P_FFN = 10, 12, 14, 18
PIECES1 = P_FFN + 3 * UNITS1

DIL = ((128, 1), (512, 4), (2048, 16))
DH = 8
SWAH, SWAKV, SWA_WIN = 16, 2, 128
NE, DE, NG, EPG = 32, 512, 4, 8
UPE = DE // CW
P_GATE, P_BRD, P_BRS, P_OUT2, P_MOE = 23, 31, 33, 37, 41
BASE2 = LAYERS * PIECES1
MOE0 = BASE2 + P_MOE
EP = 3 * UPE
CAP = P
TOP_K = 2
EXTRA = TOP_K * SEQ // (CAP + 1)
WORK = NE + EXTRA
PAIRS = (WORK + 1) // 2
PIECES = MOE0 + EP * WORK
SPLIT_AT = 960
assert WORK % 4 == 3
assert SEQ <= 2 * CAP and UPE == 2 and MOE0 % SLOTS == 2 and EP % SLOTS == 0
assert PIECES1 % SLOTS == 0

PROJ_FIRST = [0, 2, 4, 6, 8, 10, 12, 14, 16]
DURING = [[1, 3, 5], [7, 9, 11], [13, 15, 17], [18], [19], [20], [21, 22]]
PROJ_ORDER = PROJ_FIRST + [p for ps in DURING for p in ps]
PROJ_AT = {p: n for n, p in enumerate(PROJ_ORDER)}
assert sorted(PROJ_ORDER) == list(range(P_GATE))

LC_SIZES = dict(attn_g=KC, ffn_g=KC, w_small=KC * (GATES + RANK), pos_k=LP, pos_v=LP, w2_k=2 * HD,
                w2_v=2 * HD, sg_w=4 * P, sg_b=4, b_up=1)
CC_SIZES = dict(ident=P, cos_q=TT * 32, sin_q=TT * 32, cos_k=TT * 32, sin_k=TT * 32, cos_c=32, sin_c=32,
                causal=2 * P, tri=P, cmp_neg=TT * CPAD, cmp_one=TT * CPAD, dist=4 * 3 * P)
SC_SIZES = dict(mix_g=KC, ffn_g=KC, w_route=KC * (NG + NE))


def columns(sizes):
    at, out = 0, {}
    for name, n in sizes.items():
        out[name] = (at, n)
        at += n
    return out, at


LC, LC_W = columns(LC_SIZES)
CC, CC_W = columns(CC_SIZES)
SC, SC_W = columns(SC_SIZES)
R_GLA, R_LNG, R_LNB, R_W = 0, 64, 320, 576
S_BR, S_SINK, S_W = 0, NG + NE, NG + NE + SWAH

N_CROSS = TT * 2 * GH
LAYER_USES = (
    [(6 + g % 2, f"hT{g}") for g in range(4)] + [(6, "small")]
    + [(4, "z0"), (5, "z1"), (7, "aT"), (6, "gpre"), (7, "gqkT"), (4, "z2"), (5, "z3"), (4, "z4"), (5, "z5")]
    + [(n % 4, f"gs{n}") for n in range(N_CROSS + GH)]
    + [(4, "z6"), (5, "z7"), (6, "sgu"), (4, "z8"), (7, "gla"), (5, "z9"), (6, "qT0"), (7, "qT1"), (6, "kT"), (7, "cT")]
    + [(b, f"sc{u}_{b}") for u in range(4) for b in range(3)]
    + [(4, "cmpk"), (5, "cmpv")]
    + [(6 + (3 * u + j) % 2, f"pT{u}_{j}") for u in range(4) for j in range(3)]
    + [(4 + t, f"o{k}_{t}") for k in range(3) for t in range(TT)]
    + [(3, "hcT"), (3, "kc"), (3, "kcT"), (2, "cs0"), (3, "cs1"), (3, "cpT")]
    + [(6 + g % 2, f"oT{g}") for g in range(4)]
    + [(4, "w0"), (5, "w1"), (4, "w2"), (5, "w3")]
    + [(6 + g % 2, f"fT{g}") for g in range(4)]
    + [(4, f"gate{u}") for u in range(UNITS1)] + [(5, f"up{u}") for u in range(UNITS1)]
    + [(b, f"acc{b}") for b in range(4)])
SECOND_USES = (
    [(6 + g % 2, f"hT{g}") for g in range(4)]
    + [(4 + n % 2, f"z{p}") for n, p in enumerate(PROJ_FIRST)]
    + [(3, f"z{p}") for ps in DURING for p in ps]
    + [(b, f"sc{u}_{b}") for u in range(12) for b in range(3)]
    + [(6 + (3 * u + j) % 2, f"pT{u}_{j}") for u in range(12) for j in range(3)]
    + [(4 + t, f"o{k}_{t}") for k in range(3) for t in range(TT)]
    + [(4 + (p - 23) % 2, f"z{p}") for p in range(23, 31)]
    + [(6 + g % 2, f"dT{g}") for g in range(2)] + [(6 + g % 2, f"sT{g}") for g in range(4)]
    + [(4 + p % 2, f"bd{p}") for p in range(4)] + [(4 + p % 2, f"bs{p}") for p in range(4)]
    + [(6 + g % 2, f"mT{g}") for g in range(4)] + [(4 + p % 2, f"w{p}") for p in range(4)]
    + [(6 + g % 2, f"fT{g}") for g in range(4)] + [(6, "route"), (7, "count")]
    + [(b, f"moe{b}") for b in range(4, 8)]
    + [(b, f"acc{b}") for b in range(4)])
STREAMED = ("z", "cmpk", "cmpv", "w0", "w1", "w2", "w3", "gate", "up", "bd", "bs", "acc")


def bank_uses(uses):
    used, filled, out = [0] * 8, [0] * 8, {}
    for b, name in uses:
        out[name] = (b, used[b], filled[b])
        used[b] += 1
        if not name.startswith(STREAMED):
            filled[b] += 1
    return out, used, filled


USE1, USED1, FILLED1 = bank_uses(LAYER_USES)
USE2, USED2, FILLED2 = bank_uses(SECOND_USES)


def build_program(nc, a):
    ctx = ExitStack()
    with ctx:
        def sb(name, shape, dt=F32):
            return ctx.enter_context(nc.sbuf_tensor(name, shape, dt))

        def sem(name):
            return ctx.enter_context(nc.semaphore(name))

        raw = sb("raw", [P, SLOTS, PW])
        w_hi = sb("w_hi", [P, SLOTS, PW], F32R)
        w_lo = sb("w_lo", [P, SLOTS, PW], F32R)
        x = sb("x", [P, TT, D])
        nat = sb("nat", [P, TT, D])
        xT = sb("xT", [P, KC, SEQ])
        xT_hi = sb("xT_hi", [P, KC, SEQ], F32R)
        xT_lo = sb("xT_lo", [P, KC, SEQ], F32R)
        aux_r = sb("aux_r", [P, PW], F32R)
        cc = sb("cc", [P, CC_W])
        masks = sb("masks", [P, (len(LEVELS) + 1) * P], U8)
        lc = sb("lc", [P, LC_W])
        lrow = sb("lrow", [P, R_W])
        w_up = sb("w_up", [RANK, P])
        small = sb("small", [P, 512])
        row = sb("row", [P, D])
        srow = sb("srow", [P, S_W])[:, :]
        sc = sb("sc", [P, SC_W])
        extra_ids = sb("extra_ids", [P, EXTRA], I32)
        with nc.sbuf_tensor("arena", [P, ARENA], F32) as arena:
            pass
        with nc.sbuf_tensor("expert_r", [P, EXPERT_R], F32R) as expert_r:
            pass
        bank = [ctx.enter_context(nc.psum_tensor(f"bank{b}", [P, 512], F32)) for b in range(8)]

        def const(name):
            at, n = CC[name]
            return cc[:, at:at + n]

        def layer_const(name):
            at, n = LC[name]
            return lc[:, at:at + n]

        ident = const("ident")
        at_ = [0]

        def place(n, start=None):
            s = at_[0] if start is None else start
            at_[0] = s + n
            assert at_[0] <= ARENA, at_[0]
            return arena[:, s:s + n]

        cur = [0]

        def tiny(n):
            cur[0] += n
            assert cur[0] <= 512
            return small[:, cur[0] - n:cur[0]]

        wait_carrier = tiny(1)
        eps_t, sumsq, rms, rstd = tiny(1), tiny(TT), tiny(TT), tiny(TT)
        neg_max = tiny(2 * 8)
        sums = tiny(48)
        rsum = tiny(48)
        coef = tiny(32)
        g_sum, g_rms, g_rstd = tiny(8), tiny(8), tiny(8)
        bn, mv, s_rms, s_rstd = tiny(12), tiny(4), tiny(2), tiny(2)
        c_max, c_sum, c_coef = tiny(16), tiny(16), tiny(16)
        gates = tiny(TT * GATES)
        sink_e = tiny(32)
        route_t = tiny(64)

        z = place(TT * ZW).rearrange("p (t c) -> p t c", t=TT)
        qT = place(4 * SEQ).rearrange("p (c t) -> p c t", c=4)
        kTa = xT[:, 6:8, :]
        kTb = xT[:, 0:2, :]
        shared = at_[0]
        E = place(8 * SEQ)
        QE = place(8 * SEQ)
        blkf = place(LP * 64, shared)
        Sb = place(2 * 1536).rearrange("p (b n) -> p b n", b=2)
        assert at_[0] == shared + 4096
        pT = place(1536)
        AT = arena[:, at_[0] - 1536:at_[0]].rearrange("p (b n) -> p b n", b=3)
        hid = place(2 * CMP_HIDDEN).rearrange("p (k n) -> p k n", k=2)
        gq, gk = arena[:, at_[0] - 512:at_[0] - 256], arena[:, at_[0] - 256:at_[0]]
        aT = hsh = place(SEQ)
        cS = place(512)
        gx, gmin = cS[:, 0:SEQ], cS[:, SEQ:2 * SEQ]
        cpT = place(512).rearrange("p (c n) -> p c n", c=4)
        gabs, gcum = cpT[:, 0:2, :].rearrange("p c n -> p (c n)"), cpT[:, 2:4, :].rearrange("p c n -> p (c n)")
        ones = place(SEQ)
        zs = place(TT * (GATES + RANK)).rearrange("p (t c) -> p t c", t=TT)
        vbd = place(2 * 256).rearrange("p (g n) -> p g n", g=2)
        t1, t2 = place(512), place(512)
        go = t2
        swm = place(512)
        act_f, act_s = place(512, 0), place(512)
        qr = xT[:, 0:4, :].rearrange("p c t -> p (c t)").rearrange("p (t n) -> p t n", t=TT)
        kr = xT[:, 4:6, :].rearrange("p c t -> p (c t)").rearrange("p (t k n) -> p t k n", t=TT, k=2)
        hcT = xT[:, 2, :].rearrange("p (c n) -> p c n", c=4)
        kcn, kcT = xT[:, 3, 0:2 * HD], xT[:, 3, 128:192]
        blk_r = aux_r[:, :].rearrange("p (l n) -> p l n", l=LP)
        a_hi = aux_r[:, 0:512].rearrange("p (c n) -> p c n", c=2)
        a_lo = aux_r[:, 512:1024].rearrange("p (c n) -> p c n", c=2)

        vd = place(TT * 1536, 0).rearrange("p (t c) -> p t c", t=TT)
        vs = lc[:, 512:768].rearrange("p (t c) -> p t c", t=TT)
        qTd = place(12 * SEQ).rearrange("p (c t) -> p c t", c=12)
        kTd = place(12 * SEQ).rearrange("p (c t) -> p c t", c=12)
        qTs = place(8 * SEQ).rearrange("p (c t) -> p c t", c=8)
        kTs = lc[:, 0:512].rearrange("p (c t) -> p c t", c=2)
        Sb2 = place(2 * 1536).rearrange("p (b n) -> p b n", b=2)
        pT2 = place(1536)
        yd = xT[:, 4:8, :].rearrange("p c t -> p (c t)").rearrange("p (t c) -> p t c", t=TT)
        sig = arena[:, 0:4096].rearrange("p (t c) -> p t c", t=TT)
        mixed = arena[:, 4096:6144].rearrange("p (t c) -> p t c", t=TT)
        mtmp = arena[:, 6144:6656]
        split_at = [0]

        def place_r(n):
            split_at[0] += n
            assert split_at[0] <= EXPERT_R
            return expert_r[:, split_at[0] - n:split_at[0]]

        xg_split = [(place_r(2 * KC * CAP), place_r(2 * KC * CAP)) for _ in range(2)]
        y_hi, y_lo = place_r(D), place_r(D)
        put = place_r(SEQ)
        pick = place_r(4 * SEQ).rearrange("p (b t j) -> p b t j", b=2, t=TT)
        ident_r = place_r(P)
        xg = place(2 * 512, EXPERT_R).rearrange("p (b n) -> p b n", b=2)
        ones_p = place(P)
        rt = place(1024)
        silu_g, hid_f = place(4 * CAP), place(4 * CAP)
        slot_gate = place(TT * 2 * PAIRS).rearrange("p (t s) -> p t s", t=TT)
        slot_place = place(TT * 2 * PAIRS).rearrange("p (t s) -> p t s", t=TT)
        chosen, placed, picked = (place(TT * NE).rearrange("p (t e) -> p t e", t=TT) for _ in range(3))
        over, over_rank, over_hot, over_tmp = (place(NE) for _ in range(4))
        counts = place(3 * NE + P)
        from_one = counts[:, 3 * NE:3 * NE + P]
        extra_f = place(EXTRA)
        nat_hi = xT_hi[:, :, :].rearrange("p c t -> p (c t)").rearrange("p (t d) -> p t d", t=TT)
        nat_lo = xT_lo[:, :, :].rearrange("p c t -> p (c t)").rearrange("p (t d) -> p t d", t=TT)
        hid_hi = aux_r[:, 0:512].rearrange("p (c j) -> p c j", c=4)
        hid_lo = aux_r[:, 512:1024].rearrange("p (c j) -> p c j", c=4)
        gate_of = tiny(1)

        landed = [sem(f"raw_landed{s}") for s in range(SLOTS)]
        hi_ready, lo_ready = sem("weight_hi_ready"), sem("weight_lo_ready")
        lo_tail_ready = sem("weight_lo_tail_ready")
        released = sem("weight_slot_released")
        bank_filled = [sem(f"bank_filled{b}") for b in range(8)]
        bank_emptied = [sem(f"bank_emptied{b}") for b in range(8)]
        acts_hi, acts_ready = sem("acts_hi_ready"), sem("acts_ready")
        x_ready, rms_ready, normed = sem("x_ready"), sem("rms_ready"), sem("normed_ready")
        x_in, tables_in, masks_in = sem("x_landed"), sem("tables_landed"), sem("masks_landed")
        const_in, layer_in = sem("second_constants_landed"), sem("layer_constants_landed")
        dve_step, act_step = sem("vector_step"), sem("scalar_step")
        negmax_ready, probs_ready = sem("negmax_ready"), sem("probs_ready")
        pT_ready, pv_done = sem("pT_ready"), sem("pv_done")
        act_f_ready, act_hi_ready, act_ready = sem("act_f32_ready"), sem("act_hi_ready"), sem("act_ready")
        out_done = sem("output_stored")
        pick_ready, xg_f_ready, xg_hi_ready, xg_ready = (
            sem("pick_ready"), sem("tokens_f32_ready"), sem("tokens_hi_ready"), sem("tokens_ready"))
        hid_f_ready, hid_hi_ready, hid_ready = (
            sem("hidden_f32_ready"), sem("hidden_hi_ready"), sem("hidden_split"))
        y_hi_ready = sem("slot_output_hi_ready")
        once_sems = {}

        def once(name):
            if name not in once_sems:
                once_sems[name] = sem(name)
            return once_sems[name]

        def piece(l, i):
            return l * PIECES1 + i

        def use_of(l, name):
            second = isinstance(l, int) and l == LAYERS
            return (USE2 if second else USE1)[name]

        def wait_empty(eng, l, name):
            b, used, _ = use_of(l, name)
            eng.wait_ge(bank_emptied[b], l * USED1[b] + used + 1)
            return bank[b]

        def wait_emptied(eng, l, name):
            b, used, _ = use_of(l, name)
            eng.wait_ge(bank_emptied[b], l * USED1[b] + used + 2)

        def wait_filled(eng, l, name):
            b, _, filled = use_of(l, name)
            eng.wait_ge(bank_filled[b], l * FILLED1[b] + filled + 1)
            return bank[b]

        def fill(l, name, ins):
            ins.then_inc(bank_filled[use_of(l, name)[0]], 1)

        def empty(l, name, ins):
            ins.then_inc(bank_emptied[use_of(l, name)[0]], 1)

        def wait_piece(eng, idx):
            eng.wait_ge(released, idx + SLOTS + 1)

        acts_per_layer = 12

        def moe_piece(s, j):
            return MOE0 + EP * s - 2 + j

        def is_last(s):
            return isinstance(s, int) and s == WORK - 1

        def use_tokens(s, part):
            if isinstance(s, int) and s < 0:
                return 5 - part, s + 2
            return (5, 3 * s + 2) if part == 0 else (4, 2 * s + 3)

        def use_gate(s):
            return 4, 2 * s + 2

        def use_up(s):
            return 5, 3 * s + (2 if is_last(s) else 3)

        def use_hidden(s):
            return 5, 3 * s + (3 if is_last(s) else 4)

        def use_turned(s):
            return 6, 2 * s

        def use_output(s, half):
            return (6, 2 * s + 1) if half == 0 else (7, s)

        def moe_empty(eng, use):
            b, n = use
            eng.wait_ge(bank_emptied[b], LAYERS * USED1[b] + USE2[f"moe{b}"][1] + n + 1)
            return bank[b]

        def moe_emptied(eng, use):
            b, n = use
            eng.wait_ge(bank_emptied[b], LAYERS * USED1[b] + USE2[f"moe{b}"][1] + n + 2)

        def moe_filled(eng, b, s, hidden=False):
            if b == 6:
                n = s
            elif isinstance(s, int) and s < 0:
                n = s + 2
            elif b == 4:
                n = s + 2
            else:
                n = 2 * s + (3 if hidden and not is_last(s) else 2)
            eng.wait_ge(bank_filled[b], LAYERS * FILLED1[b] + USE2[f"moe{b}"][2] + n + 1)
            return bank[b]

        def nsa_unit(u):
            kind, par = u // 2, u % 2
            out = []
            for m in range(4):
                h = par + 2 * m
                g = h // 4
                kT = kTa if par == g else kTb
                out.append((slice(64 * par, 64 * par + 64), qT, h // 2, kT, kind,
                            z, (Z_SLC, Z_WIN)[kind] + 128 + 64 * g, h * HD))
            return out

        def swa_head(u, m):
            return (u - DH) // 2 * 8 + (u - DH) % 2 + 2 * m

        def second_unit(u):
            out = []
            if u < DH:
                for gi in range(3):
                    h = gi * DH + u
                    par = h % 2
                    out.append((slice(64 * par, 64 * par + 64), qTd, h // 2, kTd, h // 2, vd, h * HD, u * HD))
            else:
                for m in range(4):
                    h = swa_head(u, m)
                    par, g = h % 2, h // (SWAH // SWAKV)
                    out.append((slice(64 * par, 64 * par + 64), qTs, h // 2, kTs, 0 if par == g else 1,
                                vs, g * HD, (h % 8) * HD))
            return out

        def sums_at(l, u, k):
            if not (isinstance(l, int) and l == LAYERS):
                return u // 2 * 16 + (k // 4) * 8 + u % 2 + 2 * (k % 4)
            if u < 8:
                return k * 8 + u
            return 16 * (u // 2 - 3) + (k // 4) * 8 + u % 2 + 2 * (k % 4)

        def xs_at(g):
            return 4 + 2 * (g % 2) if g < 2 else 2 * (g - 2)

        block = ctx.enter_context(nc.Block())

        @block.sync
        def _(sp):
            def load(idx, s):
                sp.dma_start(raw[:, s, :], a["stream"][bass.ds(idx, 1)].rearrange("a p n -> (a p) n")
                             ).then_inc(landed[s], 16)

            sp.dma_start(x[:, :, :], a["x"].rearrange("(t p) d -> p t d", p=P)).then_inc(x_in, 16)
            sp.dma_start(cc[:, :], a["cc"]).then_inc(tables_in, 16)
            load(0, 0)
            sp.dma_start(arena[:, 0:(len(LEVELS) + 1) * P], a["masks"]).then_inc(masks_in, 16)
            for s in range(1, SLOTS):
                load(s, s)
            sp.dma_start(sc[:, :], a["sc"]).then_inc(const_in, 16)
            sp.dma_start(srow, a["srow"].broadcast_to([P, S_W])).then_inc(const_in, 16)
            sp.dma_start(row[:, :], a["rows"][0:1, :].broadcast_to([P, D])).then_inc(const_in, 16)
            rounds = MOE0 // SLOTS
            with sp.Fori(1, rounds) as r:
                for s in range(SLOTS):
                    sp.wait_ge(lo_ready, r * SLOTS + s - SLOTS + 1)
                    load(r * SLOTS + s, s)
            for idx in range(rounds * SLOTS, MOE0):
                sp.wait_ge(lo_ready, idx - SLOTS + 1)
                load(idx, idx % SLOTS)

            def load_expert(step, j, e, n, head=False):
                idx = moe_piece(step, j)
                at = sp.snap(MOE0 + EP * e + n)
                sp.wait_ge(lo_ready, idx - SLOTS + 1)
                if not head:
                    sp.wait_ge(lo_tail_ready, idx - SLOTS + 1)
                sp.dma_start(raw[:, j % SLOTS, :], a["stream"][bass.ds(at, 1)]
                             .rearrange("a p n -> (a p) n")).then_inc(landed[j % SLOTS], 16)

            def load_step(step, e, before):
                for j in range(2):
                    load_expert(step, j, e, j)
                for j in range(2):
                    load_expert(step, 2 + j, before, 4 + j)
                for j in range(2):
                    load_expert(step, 4 + j, e, 2 + j)

            for n in range(4):
                load_expert(0, 2 + n, 0, n, head=n < SLOTS)
            with sp.Fori(1, NE) as e:
                load_step(e, e, e - 1)
            sp.wait_ge(once("extra_ids_ready"), 1)
            before = NE - 1
            for o in range(EXTRA):
                e = sp.value_load(extra_ids[0:1, o:o + 1], min_val=0, max_val=NE - 1)
                load_step(NE + o, e, before)
                before = e
            for j in range(2):
                load_expert(WORK, j, before, 4 + j)
            sp.wait_ge(once("output_ready"), 2)
            sp.dma_start(a["out"].rearrange("(t p) d -> p t d", p=P), nat[:, :, :]).then_inc(out_done, 16)
            sp.wait_ge(out_done, 16)

        @block.gpsimd
        def _(pool):
            def lower(idx, s, n=PW):
                pool.wait_ge(hi_ready, idx + 1)
                pool.tensor_tensor(w_lo[:, s, 0:n], raw[:, s, 0:n], w_hi[:, s, 0:n].bitcast(F32),
                                   ALU.subtract).then_inc(lo_ready, 1)

            rounds = MOE0 // SLOTS
            with pool.Fori(0, rounds) as r:
                for s in range(SLOTS):
                    lower(r * SLOTS + s, s)
            for idx in range(rounds * SLOTS, (rounds + 1) * SLOTS):
                lower(idx, idx % SLOTS, PW if idx < MOE0 else SPLIT_AT)
            with pool.Fori(rounds + 1, PIECES // SLOTS) as r:
                for s in range(SLOTS):
                    lower(r * SLOTS + s, s, SPLIT_AT)
            for idx in range(PIECES // SLOTS * SLOTS, PIECES):
                lower(idx, idx % SLOTS, SPLIT_AT)

        @block.tensor
        def _(pe):
            pe.sem_inc(released, SLOTS)
            for b in range(8):
                pe.sem_inc(bank_emptied[b], 1)

            def three(out, stat, mov, first, last):
                pe.matmul(out, stat[0], mov[0], start=first, stop=False)
                pe.matmul(out, stat[1], mov[0], start=False, stop=False)
                return pe.matmul(out, stat[0], mov[1], start=False, stop=last)

            def weights(idx, s):
                pe.wait_ge(lo_ready, idx + 1)
                return w_hi[:, s, :], w_lo[:, s, :]

            def rows_piece(l, i, name, after=None):
                hi, lo = xT_hi, xT_lo
                out = wait_empty(pe, l, name)
                w = weights(piece(l, i), i % SLOTS)
                for t in range(TT):
                    for k in range(KC):
                        if after is not None and t == 0 and k % 2 == 0:
                            acts(l, after + k // 2 + 1)
                        ins = three(out[:, t * CW:(t + 1) * CW],
                                    (hi[:, k, t * P:(t + 1) * P], lo[:, k, t * P:(t + 1) * P]),
                                    (w[0][:, k * CW:(k + 1) * CW], w[1][:, k * CW:(k + 1) * CW]),
                                    k == 0, k == KC - 1)
                ins.then_inc(released, 1)

            def cols_piece(idx, s, out, parts=2, release=True, l=None, after=None):
                w = weights(idx, s)
                for c in range(parts):
                    for k in range(KC):
                        if after is not None and c == 0 and k % 2 == 0:
                            acts(l, after + k // 2 + 1)
                        o = k * CW + c * P
                        ins = three(out[:, c * SEQ:(c + 1) * SEQ], (w[0][:, o:o + P], w[1][:, o:o + P]),
                                    (xT_hi[:, k, :], xT_lo[:, k, :]), k == 0, k == KC - 1)
                if release:
                    ins.then_inc(released, 1)
                return w

            def transposes(l, names, src, per=2):
                for g, name in enumerate(names):
                    out = wait_empty(pe, l, name)
                    for c in range(per):
                        for t in range(TT):
                            o = (g * per + c) * P
                            ins = pe.transpose(out[:, (c * TT + t) * P:(c * TT + t + 1) * P],
                                               src[:, t, o:o + P], ident)
                    fill(l, name, ins)

            def acts(l, n):
                pe.wait_ge(acts_ready, l * acts_per_layer + n)

            def scores(l, u, unit):
                for b in range(3):
                    out = wait_empty(pe, l, f"sc{u}_{b}")
                    ms = range(len(unit)) if b == 0 else range(2 * b - 2, min(2 * b, len(unit)))
                    for j, m in enumerate(ms):
                        rows, q, qc, k, kc, *_ = unit[m]
                        n = P if b == 0 else SEQ
                        t = 0 if b == 0 else 1
                        ins = pe.matmul(out[:, j * n:(j + 1) * n], q[rows, qc, t * P:(t + 1) * P],
                                        k[rows, kc, 0:n], start=True, stop=True)
                    fill(l, f"sc{u}_{b}", ins)

            def prob_transposes(l, u, n, S):
                pe.wait_ge(probs_ready, l * 4 + u + 1)
                par = u % 2
                for j in range(3):
                    out = wait_empty(pe, l, f"pT{u}_{j}")
                    cols = n * P if j == 0 else (min(2 * j, n) - (2 * j - 2)) * SEQ
                    base = 0 if j == 0 else 512 + (j - 1) * 512
                    for c in range(cols // P):
                        ins = pe.transpose(out[:, c * P:(c + 1) * P], S[:, par, base + c * P:base + (c + 1) * P], ident)
                    fill(l, f"pT{u}_{j}", ins)

            def values(l, u, unit, pTv, outs, ends, joint):
                pe.wait_ge(pT_ready, l * 4 + u + 1)
                last = []
                for t in range(TT):
                    out = outs[t]
                    for m, (_, _, _, _, _, v, vc, oc) in enumerate(unit):
                        for jt in range(t + 1):
                            o = m * P if t == 0 else 512 + m * SEQ + jt * P
                            first = jt == 0 and (m == 0 or not joint)
                            stop = jt == t and (m == len(unit) - 1 or not joint)
                            ins = pe.matmul(out[:, oc:oc + HD], pTv[:, o:o + P], v[:, jt, vc:vc + HD],
                                            start=first, stop=stop)
                    if ends:
                        fill(l, ends[t], ins)
                    if t == 1 and not ends:
                        ins.then_inc(pv_done, 1)

            def ffn(l, base, nunits):
                def gate_up(u, which, idx, s, after=None):
                    b = 4 + which
                    used = USE1[("gate0", "up0")[which]][1]
                    pe.wait_ge(bank_emptied[b], l * USED1[b] + used + u + 1)
                    cols_piece(idx, s, bank[b], l=l, after=after)

                def down(u, first, last, idx, s):
                    if first:
                        for b in range(4):
                            wait_empty(pe, l, f"acc{b}")
                    w = weights(idx, s)
                    pe.wait_ge(act_ready, l * UNITS1 + u + 1)
                    for b in range(4):
                        t, half = b // 2, b % 2
                        for c in range(2):
                            o = c * D + half * 512
                            ins = three(bank[b][:, :],
                                        (a_hi[:, c, t * P:(t + 1) * P], a_lo[:, c, t * P:(t + 1) * P]),
                                        (w[0][:, o:o + 512], w[1][:, o:o + 512]),
                                        first and c == 0, last and c == 1)
                    ins.then_inc(released, 1)

                def unit(u, first=False):
                    i = base + 3 * u
                    s = lambda d: (base + d) % SLOTS
                    gate_up(u, 0, l * PIECES1 + i - 1, s(-1))
                    down(u - 1, first, False, l * PIECES1 + i, s(0))
                    gate_up(u, 1, l * PIECES1 + i + 1, s(1))

                gate_up(0, 0, l * PIECES1 + base, base % SLOTS, after=8)
                gate_up(0, 1, l * PIECES1 + base + 1, (base + 1) % SLOTS)
                unit(1, True)
                with pe.Fori(2, nunits) as u:
                    unit(u)
                down(nunits - 1, False, True, l * PIECES1 + base + 3 * nunits - 1, (base - 1) % SLOTS)

            pe.wait_ge(tables_in, 16)
            with pe.Fori(0, LAYERS) as l:
                pe.wait_ge(normed, l * 2 + 1)
                transposes(l, [f"hT{g}" for g in range(4)], nat)
                out = wait_empty(pe, l, "small")
                for t in range(TT):
                    for k in range(KC):
                        if t == 0 and k % 2 == 0:
                            acts(l, k // 2 + 1)
                        n = GATES + RANK
                        o = LC["w_small"][0] + k * n
                        ins = pe.matmul(out[:, t * n:(t + 1) * n], xT[:, k, t * P:(t + 1) * P], lc[:, o:o + n],
                                        start=k == 0, stop=k == KC - 1)
                fill(l, "small", ins)
                rows_piece(l, P_GQK, "z0")
                rows_piece(l, P_GV, "z1")
                pe.wait_ge(once("small_ready"), l + 1)
                out = wait_empty(pe, l, "aT")
                for t in range(TT):
                    ins = pe.transpose(out[0:RANK, t * P:(t + 1) * P], zs[:, t, GATES:GATES + RANK], ident)
                fill(l, "aT", ins)
                pe.wait_ge(once("aT_ready"), l + 1)
                out = wait_empty(pe, l, "gpre")
                fill(l, "gpre", pe.matmul(out[:, 0:SEQ], w_up[:, :], aT[0:RANK, :], start=True, stop=True))
                wait_emptied(pe, l, "z0")
                transposes(l, ["gqkT"], z[:, :, 0:256])
                rows_piece(l, P_GR, "z2")
                rows_piece(l, P_U, "z3")
                rows_piece(l, P_V, "z4")
                rows_piece(l, P_Q0, "z5")
                pe.wait_ge(once("decayed_ready"), l + 1)
                for n in range(N_CROSS):
                    t, lg, h = n // 8, n // 4 % 2, n % 4
                    rows = slice(DK * h, DK * h + DK)
                    out = wait_empty(pe, l, f"gs{n}")
                    for j in range(4):
                        lev = 4 * lg + j
                        if lev < len(LEVELS):
                            o = (lev + 1) * SEQ + t * P
                            k_, q_ = E[rows, o:o + P], QE[rows, o:o + P]
                        else:
                            k_, q_ = gk[rows, t * P:(t + 1) * P], gq[rows, t * P:(t + 1) * P]
                        ins = pe.matmul(out[:, j * P:(j + 1) * P], k_, q_, start=True, stop=True)
                    fill(l, f"gs{n}", ins)
                for h in range(GH):
                    rows = slice(DK * h, DK * h + DK)
                    out = wait_empty(pe, l, f"gs{N_CROSS + h}")
                    fill(l, f"gs{N_CROSS + h}",
                         pe.matmul(out[:, 0:P], E[rows, 0:P], QE[rows, P:SEQ], start=True, stop=True))
                rows_piece(l, P_Q1, "z6")
                rows_piece(l, P_SLC, "z7")
                pe.wait_ge(once("sgu_v_ready"), l + 1)
                out = wait_empty(pe, l, "sgu")
                for g in range(4):
                    ins = pe.matmul(out[:, g * P:(g + 1) * P], swm[:, g * P:(g + 1) * P],
                                    z[:, :, Z_V + g * 64:Z_V + g * 64 + 64], start=True, stop=True)
                fill(l, "sgu", ins)
                rows_piece(l, P_WIN, "z8")
                pe.wait_ge(once("gla_scores_ready"), l + 1)
                out = wait_empty(pe, l, "gla")
                for t in range(TT):
                    for h in range(GH):
                        oc = t * SEQ + h * DV
                        v0 = z[:, 0, Z_GV + h * DV:Z_GV + (h + 1) * DV]
                        v1 = z[:, 1, Z_GV + h * DV:Z_GV + (h + 1) * DV]
                        if t == 0:
                            ins = pe.matmul(out[:, oc:oc + DV], AT[:, 0, h * P:(h + 1) * P], v0, start=True, stop=True)
                        else:
                            pe.matmul(out[:, oc:oc + DV], AT[:, 2, h * P:(h + 1) * P], v0, start=True, stop=False)
                            ins = pe.matmul(out[:, oc:oc + DV], AT[:, 1, h * P:(h + 1) * P], v1, start=False, stop=True)
                fill(l, "gla", ins)
                rows_piece(l, P_CMP, "z9")
                pe.wait_ge(once("rope_ready"), l + 1)
                transposes(l, ["qT0", "qT1"], qr)
                out = wait_empty(pe, l, "kT")
                for k in range(2):
                    for t in range(TT):
                        ins = pe.transpose(out[:, (k * TT + t) * P:(k * TT + t + 1) * P], kr[:, t, k, :], ident)
                fill(l, "kT", ins)
                wait_emptied(pe, l, "z9")
                transposes(l, ["cT"], z[:, :, Z_KC:Z_KC + 256])
                pe.wait_ge(once("qT_ready"), l + 1)
                pe.wait_ge(once("kT_ready"), l + 1)
                units = [nsa_unit(u) for u in range(4)]

                def compress(which):
                    name, first = (("cmpk", P_CMPK), ("cmpv", P_CMPV))[which]
                    pe.wait_ge(once(("blk_k_ready", "blk_v_ready")[which]), l + 1)
                    out = wait_empty(pe, l, name)
                    for half in range(2):
                        w = weights(piece(l, first + half), (first + half) % SLOTS)
                        for j in range(8):
                            lp = half * 8 + j
                            for part in range(2):
                                ins = pe.matmul(out[:, 0:CMP_HIDDEN], blk_r[:, lp, :],
                                                w[part][:, j * CMP_HIDDEN:(j + 1) * CMP_HIDDEN],
                                                start=lp == 0 and part == 0, stop=lp == LP - 1 and part == 1)
                        ins.then_inc(released, 1)

                def out_banks(k):
                    return [wait_empty(pe, l, f"o{k}_{t}") for t in range(TT)]

                scores(l, 0, units[0])
                compress(0)
                scores(l, 1, units[1])
                prob_transposes(l, 0, 4, Sb)
                compress(1)
                o = out_banks(0)
                values(l, 0, units[0], pT, o, None, False)
                scores(l, 2, units[2])
                prob_transposes(l, 1, 4, Sb)
                pe.wait_ge(once("hidden_ready"), l + 1)
                out = wait_empty(pe, l, "hcT")
                for w_ in range(2):
                    for c in range(2):
                        ins = pe.matmul(out[:, (w_ * 2 + c) * 64:(w_ * 2 + c + 1) * 64],
                                        hid[0:64, w_, c * P:(c + 1) * P], ident[0:64, 0:64], start=True, stop=True)
                fill(l, "hcT", ins)
                values(l, 1, units[1], pT, o, ["o0_0", "o0_1"], False)
                scores(l, 3, units[3])
                prob_transposes(l, 2, 4, Sb)
                pe.wait_ge(once("hcT_ready"), l + 1)
                out = wait_empty(pe, l, "kc")
                for w_ in range(2):
                    wo = LC[("w2_k", "w2_v")[w_]][0]
                    for c in range(2):
                        ins = pe.matmul(out[0:64, w_ * HD:(w_ + 1) * HD], hcT[:, w_ * 2 + c, :],
                                        lc[:, wo + c * HD:wo + (c + 1) * HD], start=c == 0, stop=c == 1)
                fill(l, "kc", ins)
                o = out_banks(1)
                values(l, 2, units[2], pT, o, None, False)
                prob_transposes(l, 3, 4, Sb)
                pe.wait_ge(once("kcn_ready"), l + 1)
                out = wait_empty(pe, l, "kcT")
                fill(l, "kcT", pe.matmul(out[:, 0:64], kcn[0:64, :], ident[0:64, 0:64], start=True, stop=True))
                values(l, 3, units[3], pT, o, ["o1_0", "o1_1"], False)
                pe.wait_ge(once("kcT_ready"), l + 1)
                for par in range(2):
                    rows = slice(64 * par, 64 * par + 64)
                    out = wait_empty(pe, l, f"cs{par}")
                    for t in range(TT):
                        for m in range(4):
                            h = par + 2 * m
                            g = h // 4
                            oc = (t * 4 + m) * CPAD
                            ins = pe.matmul(out[:, oc:oc + CPAD], qT[rows, h // 2, t * P:(t + 1) * P],
                                            kcT[rows, g * CPAD:(g + 1) * CPAD], start=True, stop=True)
                    fill(l, f"cs{par}", ins)
                pe.wait_ge(once("cmp_probs_ready"), l + 1)
                out = wait_empty(pe, l, "cpT")
                for c in range(4):
                    ins = pe.transpose(out[:, c * P:(c + 1) * P], cS[:, c * P:(c + 1) * P], ident)
                fill(l, "cpT", ins)
                pe.wait_ge(once("cpT_ready"), l + 1)
                o = out_banks(2)
                for t in range(TT):
                    for g in range(2):
                        ins = pe.matmul(o[t][:, g * 256:(g + 1) * 256], cpT[:, t * 2 + g, :], vbd[:, g, :],
                                        start=True, stop=True)
                    fill(l, f"o2_{t}", ins)
                pe.wait_ge(once("mixers_ready"), l + 1)
                transposes(l, [f"oT{g}" for g in range(4)], nat)
                for i in range(4):
                    rows_piece(l, P_OUT + i, f"w{i}", after=None if i else 4)
                pe.wait_ge(normed, l * 2 + 2)
                transposes(l, [f"fT{g}" for g in range(4)], nat)
                ffn(l, P_FFN, UNITS1)

            l = LAYERS
            pe.wait_ge(normed, 2 * LAYERS + 1)
            transposes(l, [f"hT{g}" for g in range(4)], nat)
            def projection(p):
                at = PROJ_AT[p]
                if 12 <= p < 18:
                    rows_piece(l, at, f"z{p}")
                    return
                out = wait_empty(pe, l, f"z{p}")
                w = cols_piece(piece(l, at), at % SLOTS, out, parts=1 if p == 22 else 2, release=p != 22, l=l,
                               after=None if at else 0)
                if p == 22:
                    for t in range(TT):
                        for k in range(KC):
                            o = k * CW + P
                            ins = three(out[:, SEQ + t * P:SEQ + (t + 1) * P],
                                        (xT_hi[:, k, t * P:(t + 1) * P], xT_lo[:, k, t * P:(t + 1) * P]),
                                        (w[0][:, o:o + P], w[1][:, o:o + P]), k == 0, k == KC - 1)
                    ins.then_inc(released, 1)

            for p in PROJ_FIRST:
                projection(p)
            units = [second_unit(u) for u in range(12)]
            for p in PROJ_FIRST[-2:]:
                wait_emptied(pe, l, f"z{p}")
            scores(l, 0, units[0])
            for u in range(12):
                fills = iter(DURING[u] if u < len(DURING) else [])

                def between():
                    for p in fills:
                        projection(p)
                        break

                if u + 1 < 12:
                    if u + 1 == 4:
                        wait_emptied(pe, l, "z17")
                    if u + 1 == 8:
                        wait_emptied(pe, l, "z22")
                    scores(l, u + 1, units[u + 1])
                between()
                prob_transposes(l, u, len(units[u]), Sb2)
                between()
                k = (0, 1, 2)[0 if u < 8 else (u - 8) // 2 + 1]
                if u in (0, 8, 10):
                    o = [wait_empty(pe, l, f"o{k}_{t}") for t in range(TT)]
                ends = [f"o{k}_{t}" for t in range(TT)] if u in (7, 9, 11) else None
                values(l, u, units[u], pT2, o, ends, u < 8)
                between()
            pe.wait_ge(once("arena_free"), 1)
            for p in range(23, 31):
                rows_piece(l, p, f"z{p}")
            pe.wait_ge(once("y_ready"), 1)
            transposes(l, [f"dT{g}" for g in range(2)], yd)
            transposes(l, [f"sT{g}" for g in range(4)], nat)
            for i in range(2):
                w = weights(piece(l, P_BRD + i), (P_BRD + i) % SLOTS)
                for t in range(TT):
                    out = wait_empty(pe, l, f"bd{2 * i + t}")
                    for k in range(4):
                        if i == 0 and t == 0 and k % 2 == 0:
                            acts(l, 4 + k // 2 + 1)
                        ins = three(out[:, :], (aux_r[:, k * SEQ + t * P:k * SEQ + (t + 1) * P],
                                                aux_r[:, 1024 + k * SEQ + t * P:1024 + k * SEQ + (t + 1) * P]),
                                    (w[0][:, k * 512:(k + 1) * 512], w[1][:, k * 512:(k + 1) * 512]),
                                    k == 0, k == 3)
                    if t == 0:
                        ins.then_inc(once("branch_tile0_done"), 1)
                ins.then_inc(released, 1)
            for i in range(4):
                rows_piece(l, P_BRS + i, f"bs{i}", after=None if i else 6)
            pe.wait_ge(once("mixed_ready"), 1)
            transposes(l, [f"mT{g}" for g in range(4)], mixed)
            for i in range(4):
                rows_piece(l, P_OUT2 + i, f"w{i}", after=None if i else 10)
            pe.wait_ge(normed, 2 * LAYERS + 2)
            transposes(l, [f"fT{g}" for g in range(4)], nat)
            pe.wait_ge(once("router_input_ready"), 1)
            out = wait_empty(pe, l, "route")
            nr = NG + NE
            for t in range(TT):
                for k in range(KC):
                    o = SC["w_route"][0] + k * nr
                    ins = pe.matmul(out[:, t * nr:(t + 1) * nr], xT[:, k, t * P:(t + 1) * P], sc[:, o:o + nr],
                                    start=k == 0, stop=k == KC - 1)
            fill(l, "route", ins)
            pe.wait_ge(once("choices_ready"), 1)
            out = wait_empty(pe, l, "count")
            up_to = const("tri")
            pe.matmul(out[:, 0:NE], up_to, chosen[:, 0, :], start=True, stop=True)
            pe.matmul(out[:, NE:2 * NE], ones_p, chosen[:, 0, :], start=True, stop=False)
            pe.matmul(out[:, NE:2 * NE], up_to, chosen[:, 1, :], start=False, stop=True)
            pe.matmul(out[:, 2 * NE:3 * NE], ones_p, chosen[:, 0, :], start=True, stop=False)
            pe.matmul(out[:, 2 * NE:3 * NE], ones_p, chosen[:, 1, :], start=False, stop=True)
            fill(l, "count", pe.matmul(out[:, 3 * NE:3 * NE + P], ones_p, up_to, start=True, stop=True))

            def expert_weights(step, j):
                idx = moe_piece(step, j)
                pe.wait_ge(lo_ready, idx + 1)
                pe.wait_ge(lo_tail_ready, idx + 1)
                return w_hi[:, j % SLOTS, :], w_lo[:, j % SLOTS, :]

            def gather(s, par, part, pair, f):
                pe.wait_ge(pick_ready, pair + 1)
                out = moe_empty(pe, use_tokens(s, part))
                for c in range(2):
                    k = 2 * f + c
                    for t in range(TT):
                        for n, nat_part in enumerate((nat_hi, nat_lo)):
                            ins = pe.matmul(out[:, c * 2 * CAP:(c + 1) * 2 * CAP], nat_part[:, t, k * P:(k + 1) * P],
                                            pick[:, par, t, :], start=t == 0 and n == 0, stop=t == 1 and n == 1)
                ins.then_inc(bank_filled[5 - part], 1)

            def project(s, par, pair, odd, use, j0, step):
                pe.wait_ge(xg_ready, 4 * pair + 4)
                out = moe_empty(pe, use)
                for i in range(2):
                    w = expert_weights(step, j0 + i)
                    for k in range(KC):
                        ks = slice((2 * k + odd) * CAP, (2 * k + odd + 1) * CAP)
                        ws = slice(k * CW, (k + 1) * CW)
                        ins = three(out[:, i * CW:(i + 1) * CW],
                                    (xg_split[par][0][:, ks], xg_split[par][1][:, ks]),
                                    (w[0][:, ws], w[1][:, ws]), k == 0, k == KC - 1)
                    ins.then_inc(released, 1)

            def down_slot(s, step, j0):
                pe.wait_ge(hid_ready, s + 1)
                outs = [moe_empty(pe, use_output(s, half)) for half in range(2)]
                for i in range(2):
                    w = expert_weights(step, j0 + i)
                    for half in range(2):
                        for c in range(2):
                            o = c * D + half * 512
                            ins = three(outs[half][:, :], (hid_hi[:, 2 * i + c, :], hid_lo[:, 2 * i + c, :]),
                                        (w[0][:, o:o + 512], w[1][:, o:o + 512]),
                                        i == 0 and c == 0, i == 1 and c == 1)
                    ins.then_inc(released, 1)

            def put_back(s, first=False, last=False):
                moe_emptied(pe, use_turned(s))
                for half in range(2):
                    moe_emptied(pe, use_output(s, half))
                for b in range(4):
                    t, half = b // 2, b % 2
                    if first:
                        wait_empty(pe, l, f"acc{b}")
                    for n, y_ in enumerate((y_hi, y_lo)):
                        ins = pe.matmul(bank[b][:, :], put[:, t * P:(t + 1) * P], y_[:, half * 512:(half + 1) * 512],
                                        start=first and n == 0, stop=last and n == 1)
                return ins

            def turn(s, par, odd):
                out = moe_empty(pe, use_turned(s))
                for t in range(TT):
                    pe.matmul(out[:, t * P:(t + 1) * P], pick[:, par, t, odd * CAP:(odd + 1) * CAP], ident_r[:, :], start=True, stop=True)
                for t in range(TT):
                    g_ = slot_gate[:, t, s:s + 1] if isinstance(s, int) else slot_gate[:, t, bass.ds(s, 1)]
                    ins = pe.matmul(out[:, SEQ:SEQ + 1], pick[:, par, t, odd * CAP:(odd + 1) * CAP].bitcast(F32), g_,
                                    start=t == 0, stop=t == TT - 1)
                ins.then_inc(bank_filled[6], 1)

            def turn_hidden(s):
                pe.wait_ge(hid_f_ready, s + 1)
                out = moe_empty(pe, use_hidden(s))
                for c in range(4):
                    ins = pe.transpose(out[:, c * CAP:(c + 1) * CAP], hid_f[:, c * P:(c + 1) * P], ident)
                ins.then_inc(bank_filled[5], 1)

            def step_(s, pair, par, odd, first=False, last=False):
                project(s, par, pair, odd, use_gate(s), 2 if first else 0, s)
                if not last:
                    gather(s, 1 - par, 0, pair + 1, 2 * odd)
                if not first:
                    down_slot(s - 1, s, 2)
                if not last:
                    gather(s, 1 - par, 1, pair + 1, 2 * odd + 1)
                project(s, par, pair, odd, use_up(s), 4, s)
                if not first:
                    put_back(s - 1, first=isinstance(s, int) and s == 1)
                turn(s, par, odd)
                turn_hidden(s)

            pe.wait_ge(once("nat_split"), 1)
            for f in range(4):
                gather(f // 2 - 2, 0, f % 2, 0, f)
            step_(0, 0, 0, 0, first=True)
            step_(1, 0, 0, 1)
            with pe.Fori(0, WORK // 4) as r:
                for i in range(4):
                    step_(4 * r + (2 + i), 2 * r + (1 + i // 2), 1 - i // 2, i % 2)
            step_(WORK - 1, PAIRS - 1, (PAIRS - 1) % 2, 0, last=True)
            down_slot(WORK - 1, WORK, 0)
            put_back(WORK - 1, last=True).then_inc(once("experts_done"), 1)

        @block.scalar
        def _(act):
            step = [0]

            def then(ins):
                step[0] += 1
                ins.then_inc(act_step, 1)
                act.wait_ge(act_step, step[0])

            def upper(idx, s, landed_round):
                act.wait_ge(landed[s], 16 * landed_round)
                act.wait_ge(released, idx + 1)
                act.activation(w_hi[:, s, :], raw[:, s, :], ACT.Copy).then_inc(hi_ready, 1)

            def ahead(l, i):
                j = i + SLOTS
                upper(piece(l, j), j % SLOTS, l * (PIECES1 // SLOTS) + j // SLOTS + 1)

            def norm(l, n):
                act.wait_ge(x_ready, l * 2 + n + 1)
                for t in range(TT):
                    ins = act.activation(nat[:, t, :], x[:, t, :], ACT.Square, accum_out=sumsq[:, t:t + 1])
                then(ins)
                act.activation(rms[:, 0:TT], sumsq[:, 0:TT], ACT.Sqrt, bias=eps_t[:, 0:1],
                               scale=1.0 / D).then_inc(rms_ready, 1)

            def split_hi(l, names, n0, dst=None):
                for g, name in enumerate(names):
                    wait_emptied(act, l, name)
                    d = xT_hi[:, 2 * g:2 * g + 2, :] if dst is None else dst[:, g * 512:(g + 1) * 512]
                    s_ = xT[:, 2 * g:2 * g + 2, :]
                    if dst is not None:
                        s_ = s_.rearrange("p c t -> p (c t)")
                    act.activation(d, s_, ACT.Copy).then_inc(acts_hi, 1)
                act.wait_ge(acts_hi, l * acts_per_layer + n0 + len(names))

            def soft(l, u, n, S, joint):
                act.wait_ge(negmax_ready, l * 4 + u + 1)
                par = u % 2
                if joint:
                    spans = [(0, n * P, 0, 0), (512, n * SEQ, 4, 1)]
                else:
                    spans = ([(m * P, P, m, m) for m in range(n)]
                             + [(512 + m * SEQ, SEQ, 4 + m, 4 + m) for m in range(n)])
                for (o, w_, nm, sm) in spans:
                    acc = sums[:, sums_at(l, u, sm):sums_at(l, u, sm) + 1]
                    ins = act.activation(S[:, par, o:o + w_], S[:, par, o:o + w_], ACT.Exp,
                                         bias=neg_max[:, par * 8 + nm:par * 8 + nm + 1], accum_out=acc)
                ins.then_inc(probs_ready, 1)
                act.wait_ge(probs_ready, l * 4 + u + 1)

            def pT_evac(l, u, n, dst):
                for j in range(3):
                    src = wait_filled(act, l, f"pT{u}_{j}")
                    cols = n * P if j == 0 else (min(2 * j, n) - (2 * j - 2)) * SEQ
                    base = j * 512
                    empty(l, f"pT{u}_{j}", act.activation(dst[:, base:base + cols], src[:, 0:cols], ACT.Copy))
                    wait_emptied(act, l, f"pT{u}_{j}")
                wait_emptied(act, l, f"pT{u}_2")
                act.sem_inc(pT_ready, 1)

            def ffn(l, base, nunits):
                def gated(u):
                    if not (isinstance(u, int) and u == 0):
                        act.wait_ge(act_f_ready, l * UNITS1 + u)
                    act.activation(act_s, bank[4][:, :], ACT.Silu).then_inc(bank_emptied[4], 1)

                def hidden(u):
                    act.wait_ge(act_f_ready, l * UNITS1 + u + 1)
                    act.activation(aux_r[:, 0:512], act_f, ACT.Copy).then_inc(act_hi_ready, 1)

                def more(u, d):
                    s = (base + d) % SLOTS
                    r0 = (base + d - s) // SLOTS
                    upper(l * PIECES1 + base + 3 * u + d + SLOTS, s, l * (PIECES1 // SLOTS) + u + r0 + 2)

                def unit(u):
                    wait_piece(act, l * PIECES1 + base + 3 * u - 1)
                    gated(u)
                    more(u, -1)
                    more(u, 0)
                    hidden(u)
                    more(u, 1)

                wait_piece(act, l * PIECES1 + base)
                gated(0)
                more(0, 0)
                hidden(0)
                more(0, 1)
                unit(1)
                with act.Fori(2, nunits) as u:
                    unit(u)
                more(nunits, -1)

            def load_layer(l):
                for dst, src in ((lc[:, :], a["lc"]), (w_up[:, :], a["w_up"])):
                    act.dma_start(dst, src[bass.ds(l, 1)].rearrange("a p n -> (a p) n")).then_inc(layer_in, 16)
                act.dma_start(lrow[:, :], a["lrow"][bass.ds(l, 1)].broadcast_to([P, R_W])).then_inc(layer_in, 16)

            act.wait_ge(once("eps_ready"), 1)
            load_layer(0)
            norm(0, 0)
            for s in range(SLOTS):
                upper(s, s, 1)
            with act.Fori(0, LAYERS) as l:
                step[0] = 0
                act.sem_clear(act_step)
                split_hi(l, [f"hT{g}" for g in range(4)], 0)
                ahead(l, 0)
                ahead(l, 1)
                act.wait_ge(once("small_ready"), l + 1)
                act.activation(gates.rearrange("p (t c) -> p t c", t=TT), zs[:, :, 0:GATES],
                               ACT.Sigmoid).then_inc(once("nsa_gates_ready"), 1)
                act.wait_ge(once("nsa_gates_ready"), l + 1)
                act.wait_ge(once("gabs_ready"), l + 1)
                then(act.activation(gabs, gabs, ACT.Exp, scale=-1.0))
                act.activation(gabs, gabs, ACT.Ln, bias=1.0).then_inc(once("gln_ready"), 1)
                act.wait_ge(once("gln_ready"), l + 1)
                ahead(l, 2)
                wait_emptied(act, l, "z2")
                act.activation(z[:, :, Z_GR:Z_GR + 256], z[:, :, Z_GR:Z_GR + 256],
                               ACT.Silu).then_inc(once("silu_r_ready"), 1)
                act.wait_ge(once("silu_r_ready"), l + 1)
                ahead(l, 3)
                act.wait_ge(once("dist_ready"), l + 1)
                act.activation(QE, QE, ACT.Exp, scale=-1.0 / TAU).then_inc(once("decay_ready"), 1)
                act.wait_ge(once("decay_ready"), l + 1)
                ahead(l, 4)
                wait_emptied(act, l, "z4")
                act.activation(z[:, :, Z_U:Z_U + 512], z[:, :, Z_U:Z_U + 512],
                               ACT.Gelu_apprx_tanh).then_inc(once("gelu_ready"), 1)
                act.wait_ge(once("gelu_ready"), l + 1)
                ahead(l, 5)
                ahead(l, 6)
                act.wait_ge(once("sgu_var_ready"), l + 1)
                act.activation(s_rms, mv.rearrange("p (t c) -> p t c", c=2)[:, :, 1], ACT.Sqrt,
                               bias=eps_t[:, 0:1]).then_inc(once("sgu_rms_ready"), 1)
                act.wait_ge(once("sgu_rms_ready"), l + 1)
                ahead(l, 7)
                ahead(l, 8)
                act.wait_ge(once("gla_sum_ready"), l + 1)
                act.activation(g_rms, g_sum, ACT.Sqrt, bias=eps_t[:, 0:1],
                               scale=1.0 / DV).then_inc(once("gla_rms_ready"), 1)
                act.wait_ge(once("gla_rms_ready"), l + 1)
                ahead(l, 9)
                for c in range(2):
                    src = wait_filled(act, l, f"qT{c}")
                    empty(l, f"qT{c}", act.activation(qT[:, 2 * c:2 * c + 2, :],
                                                      src[:, :].rearrange("p (c t) -> p c t", c=2), ACT.Copy))
                    wait_emptied(act, l, f"qT{c}")
                wait_emptied(act, l, "qT1")
                wait_emptied(act, l, "qT0")
                act.sem_inc(once("qT_ready"), 1)
                act.wait_ge(once("blkf_k_ready"), l + 1)
                act.activation(blk_r[:, :, 0:64], blkf.rearrange("p (l n) -> p l n", l=LP),
                               ACT.Copy).then_inc(once("blk_hi_k"), 1)
                act.wait_ge(once("blk_hi_k"), l + 1)
                ahead(l, 10)
                soft(l, 0, 4, Sb, False)
                ahead(l, 11)
                act.wait_ge(once("blkf_v_ready"), l + 1)
                act.activation(blk_r[:, :, 0:64], blkf.rearrange("p (l n) -> p l n", l=LP),
                               ACT.Copy).then_inc(once("blk_hi_v"), 1)
                act.wait_ge(once("blk_hi_v"), l + 1)
                pT_evac(l, 0, 4, pT)
                def lower_rows(name, i):
                    wait_piece(act, piece(l, i))
                    act.activation(hsh[0:64, :], bank[USE1[name][0]][64:128, 0:CMP_HIDDEN],
                                   ACT.Copy).then_inc(once(name + "_rows"), 1)
                    act.wait_ge(once(name + "_rows"), l + 1)

                def gelu(w_, name):
                    act.wait_ge(once(name + "_sum"), l + 1)
                    return act.activation(hid[0:64, w_, :], hid[0:64, w_, :], ACT.Gelu_apprx_tanh)

                soft(l, 1, 4, Sb, False)
                lower_rows("cmpk", P_CMPK + 1)
                then(gelu(0, "cmpk"))
                ahead(l, 12)
                ahead(l, 13)
                lower_rows("cmpv", P_CMPV + 1)
                gelu(1, "cmpv").then_inc(once("hidden_ready"), 1)
                act.wait_ge(once("hidden_ready"), l + 1)
                act.wait_ge(pv_done, l * 2 + 1)
                pT_evac(l, 1, 4, pT)
                soft(l, 2, 4, Sb, False)
                src = wait_filled(act, l, "hcT")
                act.activation(hcT[:, :, :].rearrange("p c n -> p (c n)"), src[:, 0:256],
                               ACT.Copy).then_inc(bank_emptied[3], 1)
                wait_emptied(act, l, "hcT")
                act.sem_inc(once("hcT_ready"), 1)
                wait_filled(act, l, "o0_1")
                pT_evac(l, 2, 4, pT)
                soft(l, 3, 4, Sb, False)
                act.wait_ge(pv_done, l * 2 + 2)
                pT_evac(l, 3, 4, pT)
                act.wait_ge(once("cmp_shifted"), l + 1)
                act.activation(cS, cS, ACT.Exp).then_inc(once("cmp_exp_ready"), 1)
                act.wait_ge(once("cmp_exp_ready"), l + 1)
                src = wait_filled(act, l, "cpT")
                act.activation(cpT[:, :, :].rearrange("p c n -> p (c n)"), src[:, :],
                               ACT.Copy).then_inc(bank_emptied[3], 1)
                wait_emptied(act, l, "cpT")
                act.sem_inc(once("cpT_ready"), 1)
                split_hi(l, [f"oT{g}" for g in range(4)], 4)
                for i in range(4):
                    ahead(l, P_OUT + i)
                norm(l, 1)
                split_hi(l, [f"fT{g}" for g in range(4)], 8)
                ffn(l, P_FFN, UNITS1)
                load_layer(1)
                norm(l + 1, 0)

            l = LAYERS
            step[0] = 0
            act.sem_clear(act_step)
            norm(l, 1)
            act.dma_start(row[:, :], a["rows"][1:2, :].broadcast_to([P, D])).then_inc(const_in, 16)
            split_hi(l, [f"hT{g}" for g in range(4)], 0)
            for i in range(len(PROJ_FIRST)):
                ahead(l, i)
            for u in range(12):
                n = 3 if u < 8 else 4
                fills = DURING[u] if u < len(DURING) else []
                soft(l, u, n, Sb2, u < 8)
                for p in fills[:1]:
                    ahead(l, PROJ_AT[p])
                if u >= 8:
                    q = (u - 8) % 4
                    act.wait_ge(once("sink_diff"), u - 7)
                    act.activation(sink_e[:, q * 8:q * 8 + 8], sink_e[:, q * 8:q * 8 + 8],
                                   ACT.Exp).then_inc(once("sink_exp"), 1)
                    act.wait_ge(once("sink_exp"), u - 7)
                if u > 0:
                    if u - 1 in (7, 9):
                        wait_filled(act, l, {7: "o0_1", 9: "o1_1"}[u - 1])
                    else:
                        act.wait_ge(pv_done, LAYERS * 2 + len([v for v in range(u) if v not in (7, 9, 11)]))
                pT_evac(l, u, n, pT2)
                for p in fills[1:]:
                    ahead(l, PROJ_AT[p])
            for p in range(23, 31):
                wait_piece(act, piece(l, p))
                c0 = (p - 23) * CW
                src = bank[USE2[f"z{p}"][0]]
                empty(l, f"z{p}", act.activation(sig[:, :, c0:c0 + CW],
                                                 src[:, :].rearrange("p (t c) -> p t c", t=TT), ACT.Sigmoid))
                wait_emptied(act, l, f"z{p}")
                ahead(l, p)
            split_hi(l, ["dT0", "dT1"], 4, aux_r)
            for g in range(4):
                name = f"sT{g}"
                wait_emptied(act, l, name)
                act.activation(xT_hi[:, 2 * g:2 * g + 2, :], xT[:, xs_at(g):xs_at(g) + 2, :],
                               ACT.Copy).then_inc(acts_hi, 1)
            for i in range(31, 37):
                ahead(l, i)
            split_hi(l, [f"mT{g}" for g in range(4)], 10)
            for i in range(37, 41):
                ahead(l, i)
            norm(l, 2)
            act.wait_ge(normed, 2 * LAYERS + 2)
            act.activation(nat_hi, nat[:, :, :], ACT.Copy).then_inc(once("nat_hi_ready"), 1)
            act.wait_ge(once("nat_hi_ready"), 1)
            act.activation(ident_r, ident, ACT.Copy).then_inc(once("ident_ready"), 1)
            act.wait_ge(once("ident_ready"), 1)
            act.wait_ge(once("route_shifted"), 1)
            act.activation(rt[:, 0:72], rt[:, 0:72], ACT.Exp).then_inc(once("route_exp"), 1)
            act.wait_ge(once("route_exp"), 1)

            def upper_next(s, j):
                idx = moe_piece(s, j)
                round_ = (MOE0 - 2 + j + SLOTS) // SLOTS + 1 + EP // SLOTS * s
                act.wait_ge(landed[j % SLOTS], 16 * round_)
                act.wait_ge(released, idx + SLOTS + 1)
                act.activation(w_hi[:, j % SLOTS, :], raw[:, j % SLOTS, :], ACT.Copy).then_inc(hi_ready, 1)

            def tokens_hi(s, par, part, f):
                act.wait_ge(xg_f_ready, 2 * s + (5 + part))
                act.activation(xg_split[par][0][:, f * 512:(f + 1) * 512], xg[:, part, :],
                               ACT.Copy).then_inc(xg_hi_ready, 1)

            def turned(s):
                src = moe_filled(act, 6, s)
                act.activation(put, src[:, 0:SEQ], ACT.Copy)
                act.activation(gate_of, src[:, SEQ:SEQ + 1], ACT.Copy).then_inc(bank_emptied[6], 1)
                moe_emptied(act, use_turned(s))

            def hidden_hi(s):
                src = moe_filled(act, 5, s, hidden=True)
                act.activation(aux_r[:, 0:512], src[:, :], ACT.Copy).then_inc(hid_hi_ready, 1)

            def output_hi(s, step, j):
                wait_piece(act, moe_piece(step, j))
                for half in range(2):
                    act.activation(y_hi[:, half * 512:(half + 1) * 512], bank[6 + half][:, :], ACT.Identity,
                                   scale=gate_of[:, 0:1]).then_inc(y_hi_ready, 1)

            def step_(s, par, odd, first=False, last=False):
                g = 2 if first else 0
                if not first:
                    turned(s - 1)
                    hidden_hi(s - 1)
                upper_next(s, g)
                upper_next(s, g + 1)
                if not first:
                    act.wait_ge(hid_f_ready, s)
                act.activation(silu_g, bank[4][:, :], ACT.Silu).then_inc(bank_emptied[4], 1)
                if not first:
                    upper_next(s, 2)
                if not last:
                    tokens_hi(s, 1 - par, 0, 2 * odd)
                if not first:
                    upper_next(s, 3)
                    output_hi(s - 1, s, 3)
                if not last:
                    tokens_hi(s, 1 - par, 1, 2 * odd + 1)
                upper_next(s, 4)
                if not last:
                    upper_next(s, 5)

            for f in range(4):
                tokens_hi(f // 2 - 2, 0, f % 2, f)
            step_(0, 0, 0, first=True)
            step_(1, 0, 1)
            with act.Fori(0, WORK // 4) as r:
                for i in range(4):
                    step_(4 * r + (2 + i), 1 - i // 2, i % 2)
            step_(WORK - 1, (PAIRS - 1) % 2, 0, last=True)
            turned(WORK - 1)
            hidden_hi(WORK - 1)
            output_hi(WORK - 1, WORK, 1)
            norm(l, 3)

        @block.vector
        def _(dve):
            step = [0]

            def then(ins):
                step[0] += 1
                ins.then_inc(dve_step, 1)
                dve.wait_ge(dve_step, step[0])

            def tt(out, a_, b_, op):
                return dve.tensor_tensor(out, a_, b_, op)

            def bc(ap, axis, n):
                v = ap.unsqueeze(axis)
                shape = list(v.shape)
                shape[axis] = n
                return v.broadcast_to(shape)

            def norm(l, n):
                dve.wait_ge(rms_ready, l * 2 + n + 1)
                then(dve.reciprocal(rstd, rms))
                for t in range(TT):
                    ins = dve.tensor_scalar(nat[:, t, :], x[:, t, :], rstd[:, t:t + 1], None, ALU.mult)
                    if t == 0:
                        then(ins)
                return ins

            def split(l, names, gain, n0, hi=None, lo=None, at=None):
                total = len(names)
                base = l * acts_per_layer + n0

                def lower(g):
                    dve.wait_ge(acts_hi, base + g + 1)
                    c = 2 * g if at is None else at(g)
                    s_ = xT[:, c:c + 2, :]
                    if hi is None:
                        h_, l_ = xT_hi[:, 2 * g:2 * g + 2, :], xT_lo[:, 2 * g:2 * g + 2, :]
                    else:
                        h_, l_ = hi(g), lo(g)
                        s_ = s_.rearrange("p c t -> p (c t)")
                    tt(l_, s_, h_.bitcast(F32), ALU.subtract).then_inc(acts_ready, 1)
                    dve.wait_ge(acts_ready, base + g + 1)

                for g, name in enumerate(names):
                    src = wait_filled(dve, l, name)
                    c = 2 * g if at is None else at(g)
                    src = src[:, :].rearrange("p (c t) -> p c t", c=2)
                    if gain is None:
                        ins = dve.tensor_copy(xT[:, c:c + 2, :], src)
                    else:
                        ins = tt(xT[:, c:c + 2, :], src, bc(gain[:, 2 * g:2 * g + 2], 2, SEQ), ALU.mult)
                    empty(l, name, ins)
                    wait_emptied(dve, l, name)
                    if g > 0:
                        lower(g - 1)
                lower(total - 1)

            def evac_z(l, i, name):
                wait_piece(dve, piece(l, i))
                src = bank[use_of(l, name)[0]][:, :].rearrange("p (t c) -> p t c", t=TT)
                empty(l, name, dve.tensor_copy(z[:, :, i * CW:(i + 1) * CW], src))
                wait_emptied(dve, l, name)

            def maxes(l, u, n, S, joint):
                par = u % 2
                if joint:
                    dve.tensor_reduce(neg_max[:, par * 8:par * 8 + 1], S[:, par, 0:n * P], AX, ALU.max, negate=True)
                    ins = dve.tensor_reduce(neg_max[:, par * 8 + 4:par * 8 + 5], S[:, par, 512:512 + n * SEQ], AX,
                                            ALU.max, negate=True)
                else:
                    dve.tensor_reduce(neg_max[:, par * 8:par * 8 + n],
                                      S[:, par, 0:n * P].rearrange("p (m j) -> p m j", m=n), AX, ALU.max, negate=True)
                    ins = dve.tensor_reduce(neg_max[:, par * 8 + 4:par * 8 + 4 + n],
                                            S[:, par, 512:512 + n * SEQ].rearrange("p (m j) -> p m j", m=n), AX,
                                            ALU.max, negate=True)
                return ins

            def nsa_mask(l, u):
                par = u % 2
                if u >= 2:
                    wait_filled(dve, l, f"pT{u - 2}_2")
                causal = const("causal")
                for b in range(3):
                    src = wait_filled(dve, l, f"sc{u}_{b}")
                    n = P if b == 0 else SEQ
                    m = 512 // n
                    msk = causal[:, P:2 * P] if b == 0 else causal
                    ins = tt(Sb[:, par, b * 512:(b + 1) * 512].rearrange("p (m j) -> p m j", m=m),
                             src[:, :].rearrange("p (m j) -> p m j", m=m), bc(msk, 1, m), ALU.add)
                    empty(l, f"sc{u}_{b}", ins)
                    wait_emptied(dve, l, f"sc{u}_{b}")
                for b in range(3):
                    wait_emptied(dve, l, f"sc{u}_{b}")
                maxes(l, u, 4, Sb, False).then_inc(negmax_ready, 1)
                dve.wait_ge(negmax_ready, l * 4 + u + 1)

            def nsa_out(l, kind):
                g3 = gates.rearrange("p (n c) -> p n c", c=3)
                if kind < 2:
                    dve.wait_ge(probs_ready, l * 4 + 2 * kind + 2)
                    then(dve.reciprocal(rsum[:, kind * 16:kind * 16 + 16], sums[:, kind * 16:kind * 16 + 16]))
                    then(tt(coef[:, kind * 16:kind * 16 + 16], rsum[:, kind * 16:kind * 16 + 16],
                            g3[:, :, kind + 1], ALU.mult))
                for t in range(TT):
                    src = wait_filled(dve, l, f"o{kind}_{t}")
                    dst = nat[:, t, 0:512]
                    if kind == 2:
                        empty(l, f"o2_{t}", tt(dst, src[:, :], dst, ALU.add))
                        wait_emptied(dve, l, f"o2_{t}")
                        continue
                    s3 = src[:, :].rearrange("p (h d) -> p h d", h=8)
                    c3 = bc(coef[:, kind * 16 + t * 8:kind * 16 + t * 8 + 8], 2, HD)
                    if kind == 0:
                        empty(l, f"o0_{t}", tt(dst.rearrange("p (h d) -> p h d", h=8), s3, c3, ALU.mult))
                        wait_emptied(dve, l, f"o0_{t}")
                    else:
                        empty(l, f"o1_{t}", tt(t1.rearrange("p (h d) -> p h d", h=8), s3, c3, ALU.mult))
                        wait_emptied(dve, l, f"o1_{t}")
                        wait_emptied(dve, l, f"o1_{t}")
                        then(tt(dst, dst, t1, ALU.add))

            def residual(l, names, i0):
                for i, name in enumerate(names):
                    wait_piece(dve, piece(l, i0 + i))
                    src = bank[use_of(l, name)[0]][:, :].rearrange("p (t c) -> p t c", t=TT)
                    xs_ = x[:, :, i * CW:(i + 1) * CW]
                    empty(l, name, tt(xs_, src, xs_, ALU.add))
                    wait_emptied(dve, l, name)
                for name in names[-2:]:
                    wait_emptied(dve, l, name)
                dve.sem_inc(x_ready, 1)

            def ffn(l, base, nunits):
                def unit(u):
                    dve.wait_ge(bank_emptied[4], l * USED1[4] + USE1["gate0"][1] + u + 2)
                    wait_piece(dve, l * PIECES1 + base + 3 * u + 1)
                    if not (isinstance(u, int) and u == 0):
                        dve.wait_ge(act_ready, l * UNITS1 + u)
                    dve.tensor_tensor(act_f, bank[5][:, :], act_s, ALU.mult).then_inc(bank_emptied[5], 1)
                    dve.wait_ge(bank_emptied[5], l * USED1[5] + USE1["up0"][1] + u + 2)
                    dve.sem_inc(act_f_ready, 1)
                    dve.wait_ge(act_hi_ready, l * UNITS1 + u + 1)
                    dve.tensor_tensor(aux_r[:, 512:1024], act_f, aux_r[:, 0:512].bitcast(F32),
                                      ALU.subtract).then_inc(act_ready, 1)

                unit(0)
                unit(1)
                with dve.Fori(2, nunits) as u:
                    unit(u)
                add_output(l, lambda: wait_piece(dve, l * PIECES1 + base + 3 * nunits - 1))

            def add_output(l, done):
                done()
                for b in range(4):
                    t, half = b // 2, b % 2
                    xs_ = x[:, t, half * 512:(half + 1) * 512]
                    empty(l, f"acc{b}", tt(xs_, bank[b][:, :], xs_, ALU.add))
                    wait_emptied(dve, l, f"acc{b}")
                for b in range(4):
                    wait_emptied(dve, l, f"acc{b}")
                dve.sem_inc(x_ready, 1)

            dve.sem_inc(lo_tail_ready, MOE0)
            then(dve.memset(eps_t, EPS))
            dve.memset(ones, 1.0).then_inc(once("eps_ready"), 1)
            dve.wait_ge(once("eps_ready"), 1)
            dve.memset(vbd[:, :, :], 0.0).then_inc(once("vbd_zero"), 1)
            dve.wait_ge(once("vbd_zero"), 1)
            dve.wait_ge(x_in, 16)
            dve.sem_inc(x_ready, 1)
            dve.wait_ge(masks_in, 16)
            then(dve.tensor_copy(masks[:, :], arena[:, 0:(len(LEVELS) + 1) * P]))
            dve.wait_ge(tables_in, 16)
            with dve.Fori(0, LAYERS) as l:
                step[0] = 0
                dve.sem_clear(dve_step)
                norm(l, 0).then_inc(normed, 1)
                dve.wait_ge(layer_in, l * 48 + 48)
                split(l, [f"hT{g}" for g in range(4)], layer_const("attn_g"), 0)
                then(tt(swm.rearrange("p (g i) -> p g i", g=4),
                        layer_const("sg_w").rearrange("p (g i) -> p g i", g=4), bc(const("tri"), 1, 4), ALU.mult))
                src = wait_filled(dve, l, "small")
                empty(l, "small", dve.tensor_copy(
                    zs[:, :, :], src[:, 0:TT * (GATES + RANK)].rearrange("p (t c) -> p t c", t=TT)))
                wait_emptied(dve, l, "small")
                wait_emptied(dve, l, "small")
                dve.sem_inc(once("small_ready"), 1)
                evac_z(l, 0, "z0")
                evac_z(l, 1, "z1")
                src = wait_filled(dve, l, "aT")
                empty(l, "aT", dve.tensor_copy(aT[0:RANK, :], src[0:RANK, 0:SEQ]))
                wait_emptied(dve, l, "aT")
                wait_emptied(dve, l, "aT")
                dve.sem_inc(once("aT_ready"), 1)
                src = wait_filled(dve, l, "gpre")
                empty(l, "gpre", dve.tensor_scalar(gx, src[:, 0:SEQ], layer_const("b_up"), None, ALU.add))
                wait_emptied(dve, l, "gpre")
                wait_emptied(dve, l, "gpre")
                then(dve.tensor_scalar(gmin, gx, 0.0, None, ALU.min))
                dve.scalar_tensor_tensor(gabs, gx, -1.0, gx, ALU.mult, ALU.max).then_inc(once("gabs_ready"), 1)
                dve.wait_ge(once("gabs_ready"), l + 1)
                src = wait_filled(dve, l, "gqkT")
                then(dve.tensor_scalar(gq, src[:, 0:SEQ], DK ** -0.5, None, ALU.mult))
                empty(l, "gqkT", dve.tensor_copy(gk, src[:, SEQ:2 * SEQ]))
                wait_emptied(dve, l, "gqkT")
                evac_z(l, 2, "z2")
                dve.wait_ge(once("gln_ready"), l + 1)
                then(tt(gmin, gmin, gabs, ALU.subtract))
                then(dve.tensor_tensor_scan(gcum, ones, gmin, 0.0, ALU.mult, ALU.add))
                for n, s in enumerate([P] + LEVELS):
                    nb = SEQ // (2 * s)
                    cv = gcum.rearrange("p (b s) -> p b s", b=nb)
                    ins = tt(E[:, n * SEQ:(n + 1) * SEQ].rearrange("p (b s) -> p b s", b=nb), cv,
                             cv[:, :, s - 1:s].broadcast_to([P, nb, 2 * s]), ALU.subtract)
                then(ins)
                dve.scalar_tensor_tensor(QE, E, -1.0, E, ALU.mult, ALU.max).then_inc(once("dist_ready"), 1)
                dve.wait_ge(once("dist_ready"), l + 1)
                evac_z(l, 3, "z3")
                evac_z(l, 4, "z4")
                dve.wait_ge(once("decay_ready"), l + 1)
                lv = "p (n t) -> p n t"
                then(tt(E.rearrange(lv, n=8), QE.rearrange(lv, n=8), bc(gk, 1, 8), ALU.mult))
                tt(QE.rearrange(lv, n=8), QE.rearrange(lv, n=8), bc(gq, 1, 8), ALU.mult).then_inc(once("decayed_ready"), 1)
                dve.wait_ge(once("decayed_ready"), l + 1)
                evac_z(l, 5, "z5")
                then(dve.memset(AT[:, 0:2, :], 0.0))
                for n in range(N_CROSS):
                    t, lg, h = n // 8, n // 4 % 2, n % 4
                    src = wait_filled(dve, l, f"gs{n}")
                    then(dve.memset(wait_carrier, 0.0))
                    for j in range(4):
                        lev = 4 * lg + j
                        ins = dve.copy_predicated(AT[:, t, h * P:(h + 1) * P], masks[:, lev * P:(lev + 1) * P],
                                                  src[:, j * P:(j + 1) * P])
                        if j < 3:
                            then(ins)
                    empty(l, f"gs{n}", ins)
                    wait_emptied(dve, l, f"gs{n}")
                for h in range(GH):
                    src = wait_filled(dve, l, f"gs{N_CROSS + h}")
                    empty(l, f"gs{N_CROSS + h}", dve.tensor_copy(AT[:, 2, h * P:(h + 1) * P], src[:, 0:P]))
                    wait_emptied(dve, l, f"gs{N_CROSS + h}")
                for h in range(GH):
                    wait_emptied(dve, l, f"gs{N_CROSS + h}")
                dve.sem_inc(once("gla_scores_ready"), 1)
                dve.wait_ge(once("gelu_ready"), l + 1)
                for t in range(TT):
                    then(dve.bn_stats(bn[:, t * 6:t * 6 + 6], z[:, t, Z_V:Z_V + 256]))
                    ins = dve.bn_aggr(mv[:, t * 2:t * 2 + 2], bn[:, t * 6:t * 6 + 6])
                    if t == 0:
                        then(ins)
                ins.then_inc(once("sgu_var_ready"), 1)
                dve.wait_ge(once("sgu_var_ready"), l + 1)
                evac_z(l, 6, "z6")
                dve.wait_ge(once("sgu_rms_ready"), l + 1)
                then(dve.reciprocal(s_rstd, s_rms))
                for t in range(TT):
                    v_ = z[:, t, Z_V:Z_V + 256]
                    then(dve.tensor_scalar(v_, v_, mv[:, 2 * t:2 * t + 1], s_rstd[:, t:t + 1], ALU.subtract, ALU.mult))
                v_ = z[:, :, Z_V:Z_V + 256]
                then(tt(v_, v_, bc(lrow[:, R_LNG:R_LNG + 256], 1, TT), ALU.mult))
                tt(v_, v_, bc(lrow[:, R_LNB:R_LNB + 256], 1, TT), ALU.add).then_inc(once("sgu_v_ready"), 1)
                dve.wait_ge(once("sgu_v_ready"), l + 1)
                evac_z(l, 7, "z7")
                src = wait_filled(dve, l, "sgu")
                for g in range(4):
                    c = 768 + g * 64
                    ins = dve.scalar_tensor_tensor(
                        nat[:, :, c:c + 64], src[:, g * P:(g + 1) * P].rearrange("p (t c) -> p t c", t=TT),
                        layer_const("sg_b")[:, g:g + 1], z[:, :, Z_U + g * 64:Z_U + (g + 1) * 64], ALU.add, ALU.mult)
                empty(l, "sgu", ins)
                wait_emptied(dve, l, "sgu")
                rr = "p (t f) -> p t f"

                def rope(dst1, dst2, x1, x2, cos, sin, nh):
                    c_ = bc(const(cos).rearrange(rr, t=TT), 2, nh)
                    s_ = bc(const(sin).rearrange(rr, t=TT), 2, nh)
                    a_, b_ = (v[:, 0:TT * nh * 32].rearrange("p (t h f) -> p t h f", t=TT, h=nh) for v in (t1, t2))
                    tt(a_, x1, c_, ALU.mult)
                    then(tt(b_, x2, s_, ALU.mult))
                    then(tt(dst1, a_, b_, ALU.subtract))
                    tt(a_, x2, c_, ALU.mult)
                    then(tt(b_, x1, s_, ALU.mult))
                    return tt(dst2, a_, b_, ALU.add)

                def halves(v, nh):
                    v = v.rearrange("p t (h f) -> p t h f", h=nh)
                    return v[:, :, :, 0:32], v[:, :, :, 32:64]

                wait_emptied(dve, l, "z6")
                then(rope(*halves(qr, 8), *halves(z[:, :, Z_Q:Z_Q + 512], 8), "cos_q", "sin_q", 8))
                evac_z(l, 8, "z8")
                wait_emptied(dve, l, "z8")
                wait_emptied(dve, l, "z7")
                for k, c in enumerate((Z_SLC, Z_WIN)):
                    ins = rope(*halves(kr[:, :, k, :], 2), *halves(z[:, :, c:c + 128], 2), "cos_k", "sin_k", 2)
                    if k == 0:
                        then(ins)
                ins.then_inc(once("rope_ready"), 1)
                dve.wait_ge(once("rope_ready"), l + 1)
                src = wait_filled(dve, l, "gla")
                empty(l, "gla", dve.tensor_copy(go, src[:, :]))
                wait_emptied(dve, l, "gla")
                wait_emptied(dve, l, "gla")
                then(tt(t1, go, go, ALU.mult))
                h8 = "p (n d) -> p n d"
                dve.tensor_reduce(g_sum, t1.rearrange(h8, n=8), AX, ALU.add).then_inc(once("gla_sum_ready"), 1)
                dve.wait_ge(once("gla_sum_ready"), l + 1)
                evac_z(l, 9, "z9")
                src = wait_filled(dve, l, "kT")
                flat = lambda v: v.rearrange("p c t -> p (c t)")
                dve.tensor_copy(flat(kTa), src[:, :])
                dve.tensor_copy(flat(kTb)[0:64, :], src[64:128, :])
                empty(l, "kT", dve.tensor_copy(flat(kTb)[64:128, :], src[0:64, :]))
                wait_emptied(dve, l, "kT")
                wait_emptied(dve, l, "kT")
                dve.sem_inc(once("kT_ready"), 1)
                src = wait_filled(dve, l, "cT")
                b3 = blkf.rearrange("p (l n) -> p l n", l=LP)

                def blocks(which):
                    pos = layer_const(("pos_k", "pos_v")[which])
                    if which:
                        wait_piece(dve, piece(l, P_CMPK + 1))
                    if not which:
                        for g in range(2):
                            dve.memset(b3[:, :, g * CPAD + NCMP:(g + 1) * CPAD], 0.0)
                    for par in range(2):
                        for g in range(2):
                            rows = slice(64 * par, 64 * par + 64)
                            s_ = src[64 * g:64 * g + 64, which * SEQ:(which + 1) * SEQ]
                            s_ = s_.rearrange("p (c s) -> p s c", s=CMP_STRIDE)
                            for hf in range(2):
                                o_ = b3[rows, hf * 8:(hf + 1) * 8, g * CPAD:g * CPAD + NCMP]
                                i_ = s_[:, par:CMP_STRIDE:2, hf:hf + NCMP]
                                p_ = bc(pos[rows, hf * 8:(hf + 1) * 8], 2, NCMP)
                                ins = tt(o_, i_, p_, ALU.add)
                    ins.then_inc(once(("blkf_k_ready", "blkf_v_ready")[which]), 1)
                    dve.wait_ge(once(("blkf_k_ready", "blkf_v_ready")[which]), l + 1)

                def block_low(which):
                    dve.wait_ge(once(("blk_hi_k", "blk_hi_v")[which]), l + 1)
                    tt(blk_r[:, :, 64:128], b3, blk_r[:, :, 0:64].bitcast(F32),
                       ALU.subtract).then_inc(once(("blk_k_ready", "blk_v_ready")[which]), 1)
                    dve.wait_ge(once(("blk_k_ready", "blk_v_ready")[which]), l + 1)

                blocks(0)
                block_low(0)
                dve.wait_ge(once("gla_rms_ready"), l + 1)
                then(dve.reciprocal(g_rstd, g_rms))
                then(tt(go.rearrange(h8, n=8), go.rearrange(h8, n=8), bc(g_rstd, 2, DV), ALU.mult))
                then(tt(go.rearrange(h8, n=8), go.rearrange(h8, n=8), bc(lrow[:, R_GLA:R_GLA + 64], 1, 8), ALU.mult))
                dve.wait_ge(once("silu_r_ready"), l + 1)
                then(tt(nat[:, :, 512:768], go.rearrange("p (t c) -> p t c", t=TT), z[:, :, Z_GR:Z_GR + 256], ALU.mult))
                nsa_mask(l, 0)
                blocks(1)
                dve.wait_ge(once("blkf_v_ready"), l + 1)
                dve.sem_inc(bank_emptied[USE1["cT"][0]], 1)
                block_low(1)
                nsa_mask(l, 1)

                def hidden(w_, name):
                    dve.wait_ge(once(name + "_rows"), l + 1)
                    empty(l, name, tt(hid[0:64, w_, :], bank[USE1[name][0]][0:64, 0:CMP_HIDDEN], hsh[0:64, :], ALU.add))
                    wait_emptied(dve, l, name)
                    wait_emptied(dve, l, name)
                    dve.sem_inc(once(name + "_sum"), 1)

                hidden(0, "cmpk")
                hidden(1, "cmpv")
                nsa_mask(l, 2)
                dve.wait_ge(once("nsa_gates_ready"), l + 1)
                nsa_out(l, 0)
                nsa_mask(l, 3)
                src = wait_filled(dve, l, "kc")
                cc_, cs_ = const("cos_c")[0:64, :], const("sin_c")[0:64, :]
                k1, k2 = src[0:64, 0:32], src[0:64, 32:64]
                a_, b_ = t1[0:64, 0:32], t2[0:64, 0:32]
                tt(a_, k1, cc_, ALU.mult)
                then(tt(b_, k2, cs_, ALU.mult))
                then(tt(kcn[0:64, 0:32], a_, b_, ALU.subtract))
                tt(a_, k2, cc_, ALU.mult)
                then(tt(b_, k1, cs_, ALU.mult))
                then(tt(kcn[0:64, 32:64], a_, b_, ALU.add))
                dve.tensor_copy(kcn[0:64, HD:2 * HD], kcn[0:64, 0:HD]).then_inc(once("kcn_ready"), 1)
                dve.wait_ge(once("kcn_ready"), l + 1)
                for g in range(2):
                    for m in range(4):
                        ins = dve.tensor_copy(vbd[m * 32:(m + 1) * 32, g, m * HD:(m + 1) * HD],
                                              src[g * 32:(g + 1) * 32, HD:2 * HD])
                empty(l, "kc", ins)
                wait_emptied(dve, l, "kc")
                src = wait_filled(dve, l, "kcT")
                empty(l, "kcT", dve.tensor_copy(kcT[:, :], src[:, 0:64]))
                wait_emptied(dve, l, "kcT")
                wait_emptied(dve, l, "kcT")
                dve.sem_inc(once("kcT_ready"), 1)
                nsa_out(l, 1)
                v4 = "p (t h c) -> p t h c"
                cneg = const("cmp_neg").rearrange("p (t c) -> p t c", t=TT)
                c1 = bc(const("cmp_one").rearrange("p (t c) -> p t c", t=TT), 2, HEADS)
                S4, S3 = cS.rearrange(v4, t=TT, h=HEADS), cS.rearrange("p (n c) -> p n c", c=CPAD)
                for par in range(2):
                    src = wait_filled(dve, l, f"cs{par}")
                    empty(l, f"cs{par}", tt(S4[:, :, par:HEADS:2, :], src[:, 0:256].rearrange(v4, t=TT, h=4),
                                            bc(cneg, 2, 4), ALU.add))
                    wait_emptied(dve, l, f"cs{par}")
                    wait_emptied(dve, l, f"cs{par}")
                then(dve.tensor_reduce(c_max, S3, AX, ALU.max, negate=True))
                tt(S3, S3, bc(c_max, 2, CPAD), ALU.add).then_inc(once("cmp_shifted"), 1)
                dve.wait_ge(once("cmp_exp_ready"), l + 1)
                then(tt(S4, S4, c1, ALU.mult))
                then(dve.tensor_reduce(c_sum, S3, AX, ALU.add))
                then(dve.tensor_scalar(c_sum, c_sum, 1e-30, None, ALU.max))
                then(dve.reciprocal(c_sum, c_sum))
                then(tt(c_coef, c_sum, gates.rearrange("p (n c) -> p n c", c=3)[:, :, 0], ALU.mult))
                tt(S3, S3, bc(c_coef, 2, CPAD), ALU.mult).then_inc(once("cmp_probs_ready"), 1)
                dve.wait_ge(once("cmp_probs_ready"), l + 1)
                nsa_out(l, 2)
                wait_emptied(dve, l, "o2_0")
                wait_emptied(dve, l, "o2_1")
                wait_emptied(dve, l, "sgu")
                dve.sem_inc(once("mixers_ready"), 1)
                split(l, [f"oT{g}" for g in range(4)], None, 4)
                residual(l, [f"w{i}" for i in range(4)], P_OUT)
                norm(l, 1).then_inc(normed, 1)
                split(l, [f"fT{g}" for g in range(4)], layer_const("ffn_g"), 8)
                ffn(l, P_FFN, UNITS1)

            l = LAYERS
            step[0] = 0
            dve.sem_clear(dve_step)
            dve.wait_ge(const_in, 16 * 3)
            dve.wait_ge(layer_in, LAYERS * 48 + 48)
            then(norm(l, 0))
            for t in range(TT):
                then(tt(x[:, t, :], nat[:, t, :], row[:, :], ALU.mult))
            dve.sem_inc(x_ready, 1)
            norm(l, 1).then_inc(normed, 1)
            sg_ = lambda name: sc[:, SC[name][0]:SC[name][0] + SC[name][1]]
            split(l, [f"hT{g}" for g in range(4)], sg_("mix_g"), 0)
            def take_projection(p):
                wait_piece(dve, piece(l, PROJ_AT[p]))
                src = bank[USE2[f"z{p}"][0]]
                if p < 12 or 18 <= p < 22:
                    dst, c = (qTd, p) if p < 6 else (kTd, p - 6) if p < 12 else (qTs, p - 18)
                    s3 = src[:, :].rearrange("p (c t) -> p c t", c=2)
                    d3 = dst[:, 2 * c:2 * c + 2, :]
                    if 6 <= p < 12:
                        ins = dve.tensor_copy(d3, s3)
                    else:
                        ins = dve.tensor_scalar(d3, s3, HD ** -0.5, None, ALU.mult)
                elif p < 18:
                    ins = dve.tensor_copy(vd[:, :, (p - 12) * CW:(p - 11) * CW],
                                          src[:, :].rearrange("p (t c) -> p t c", t=TT))
                else:
                    then(dve.tensor_copy(kTs[:, 0, :], src[:, 0:SEQ]))
                    then(dve.tensor_copy(kTs[0:64, 1, :], src[64:128, 0:SEQ]))
                    then(dve.tensor_copy(kTs[64:128, 1, :], src[0:64, 0:SEQ]))
                    ins = dve.tensor_copy(vs[:, :, :], src[:, SEQ:2 * SEQ].rearrange("p (t c) -> p t c", t=TT))
                empty(l, f"z{p}", ins)
                wait_emptied(dve, l, f"z{p}")

            for p in PROJ_FIRST:
                take_projection(p)
            slopes_d = (2.0 ** (-8.0 * np.arange(1, 25) / 24)).astype(np.float32)
            slopes_s = (2.0 ** (-8.0 * np.arange(1, 17) / 16)).astype(np.float32)

            def mask2(u):
                par = u % 2
                n = 3 if u < 8 else 4
                if u >= 2:
                    wait_filled(dve, l, f"pT{u - 2}_2")
                for b in range(3):
                    src = wait_filled(dve, l, f"sc{u}_{b}")
                    ms = range(n) if b == 0 else range(2 * b - 2, min(2 * b, n))
                    w_ = P if b == 0 else SEQ
                    for j, m in enumerate(ms):
                        d0 = CC["dist"][0] + (m if u < 8 else 3) * 3 * P + (0 if b == 0 else P)
                        slope = float(slopes_d[m * DH + u]) if u < 8 else float(slopes_s[swa_head(u, m)])
                        o = m * P if b == 0 else 512 + m * SEQ
                        ins = dve.scalar_tensor_tensor(Sb2[:, par, o:o + w_], cc[:, d0:d0 + w_], slope,
                                                       src[:, j * w_:(j + 1) * w_], ALU.mult, ALU.add)
                    empty(l, f"sc{u}_{b}", ins)
                    wait_emptied(dve, l, f"sc{u}_{b}")
                for b in range(3):
                    wait_emptied(dve, l, f"sc{u}_{b}")
                ins = maxes(l, u, n, Sb2, u < 8)
                if u < 8:
                    ins.then_inc(negmax_ready, 1)
                    dve.wait_ge(negmax_ready, LAYERS * 4 + u + 1)
                    return
                then(ins)
                q = u - 8
                nm = neg_max[:, par * 8:par * 8 + 8].rearrange("p (t m) -> p t m", t=TT)
                sk = srow[:, S_SINK + swa_head(u, 0):S_SINK + swa_head(u, 3) + 1:2]
                ng = route_t[:, 0:4]
                then(dve.tensor_scalar(ng, sk, -1.0, None, ALU.mult))
                tt(nm, nm, bc(ng, 1, TT), ALU.min).then_inc(negmax_ready, 1)
                dve.wait_ge(negmax_ready, LAYERS * 4 + u + 1)
                tt(sink_e[:, q * 8:q * 8 + 8].rearrange("p (t m) -> p t m", t=TT), nm, bc(sk, 1, TT),
                   ALU.add).then_inc(once("sink_diff"), 1)
                dve.wait_ge(once("sink_diff"), u - 7)

            def out2(k):
                u = (7, 9, 11)[k]
                dve.wait_ge(probs_ready, LAYERS * 4 + u + 1)
                s0 = 16 * k
                if k:
                    dve.wait_ge(once("sink_exp"), 2 * k)
                    for q in range(2):
                        u8 = (2 * (k - 1) + q) * 8
                        v = sums[:, s0:s0 + 16].rearrange("p (t n) -> p t n", t=TT)[:, :, q:8:2]
                        then(tt(v, v, sink_e[:, u8:u8 + 8].rearrange("p (t m) -> p t m", t=TT), ALU.add))
                dve.reciprocal(rsum[:, s0:s0 + 16], sums[:, s0:s0 + 16]).then_inc(once("sums_used"), 1)
                dve.wait_ge(once("sums_used"), k + 1)
                for t in range(TT):
                    src = wait_filled(dve, l, f"o{k}_{t}")
                    dst = yd[:, t, :] if k == 0 else nat[:, t, (k - 1) * 512:k * 512]
                    h8_ = "p (h d) -> p h d"
                    empty(l, f"o{k}_{t}", tt(dst.rearrange(h8_, h=8), src[:, :].rearrange(h8_, h=8),
                                             bc(rsum[:, s0 + t * 8:s0 + t * 8 + 8], 2, HD), ALU.mult))
                    wait_emptied(dve, l, f"o{k}_{t}")

            mask2(0)
            for u in range(12):
                if u + 1 < 12:
                    mask2(u + 1)
                for p in DURING[u] if u < len(DURING) else []:
                    take_projection(p)
                if u in (7, 9, 11):
                    out2({7: 0, 9: 1, 11: 2}[u])
            wait_emptied(dve, l, "o2_0")
            wait_emptied(dve, l, "o2_1")
            dve.sem_inc(once("arena_free"), 1)
            dve.sem_inc(once("y_ready"), 1)
            split(l, ["dT0", "dT1"], None, 4, lambda g: aux_r[:, g * 512:(g + 1) * 512],
                  lambda g: aux_r[:, 1024 + g * 512:1024 + (g + 1) * 512])
            split(l, [f"sT{g}" for g in range(4)], None, 6, at=xs_at)
            for i in range(4):
                t, half = i % 2, i // 2
                if t == 0:
                    dve.wait_ge(once("branch_tile0_done"), half + 1)
                else:
                    wait_piece(dve, piece(l, P_BRD + half))
                cs2 = slice(half * 512, half * 512 + 512)
                empty(l, f"bd{i}", tt(mixed[:, t, cs2], bank[USE2[f"bd{i}"][0]][:, :], sig[:, t, cs2], ALU.mult))
                wait_emptied(dve, l, f"bd{i}")
            wait_emptied(dve, l, "bd2")
            wait_emptied(dve, l, "bd3")
            for i in range(4):
                wait_piece(dve, piece(l, P_BRS + i))
                src = bank[USE2[f"bs{i}"][0]][:, :].rearrange("p (t c) -> p t c", t=TT)
                m3 = mtmp.rearrange("p (t c) -> p t c", t=TT)
                cs2 = slice(i * CW, (i + 1) * CW)
                empty(l, f"bs{i}", tt(m3, src, sig[:, :, D + i * CW:D + (i + 1) * CW], ALU.mult))
                wait_emptied(dve, l, f"bs{i}")
                wait_emptied(dve, l, f"bs{i}")
                then(tt(mixed[:, :, cs2], mixed[:, :, cs2], m3, ALU.add))
            dve.sem_inc(once("mixed_ready"), 1)
            split(l, [f"mT{g}" for g in range(4)], None, 10)
            residual(l, [f"w{i}" for i in range(4)], P_OUT2)
            norm(l, 2).then_inc(normed, 1)
            def lower_tail(idx, s):
                dve.wait_ge(hi_ready, idx + 1)
                tt(w_lo[:, s, SPLIT_AT:PW], raw[:, s, SPLIT_AT:PW], w_hi[:, s, SPLIT_AT:PW].bitcast(F32),
                   ALU.subtract).then_inc(lo_tail_ready, 1)

            for g in range(4):
                src = wait_filled(dve, l, f"fT{g}")
                empty(l, f"fT{g}", tt(xT[:, 2 * g:2 * g + 2, :], src[:, :].rearrange("p (c t) -> p c t", c=2),
                                      bc(sg_("ffn_g")[:, 2 * g:2 * g + 2], 2, SEQ), ALU.mult))
                wait_emptied(dve, l, f"fT{g}")
            for g in range(2, 4):
                wait_emptied(dve, l, f"fT{g}")
            dve.sem_inc(once("router_input_ready"), 1)
            dve.wait_ge(once("nat_hi_ready"), 1)
            tt(nat_lo, nat[:, :, :], nat_hi.bitcast(F32), ALU.subtract).then_inc(once("nat_split"), 1)
            dve.wait_ge(once("nat_split"), 1)
            then(dve.memset(ones_p, 1.0))
            rank = route_t[:, 0:8]
            for j in range(8):
                ins = dve.memset(rank[:, j:j + 1], float(8 - j))
            then(ins)

            nr = NG + NE
            src = wait_filled(dve, l, "route")
            lg = rt[:, 0:TT * nr].rearrange("p (t c) -> p t c", t=TT)
            br = srow[:, S_BR:S_BR + nr]
            empty(l, "route", tt(lg, src[:, 0:TT * nr].rearrange("p (t c) -> p t c", t=TT), bc(br, 1, TT), ALU.add))
            wait_emptied(dve, l, "route")
            wait_emptied(dve, l, "route")
            sl = [80]

            def room(n):
                sl[0] += n
                assert sl[0] <= 512
                return rt[:, sl[0] - n:sl[0]].rearrange("p (t n) -> p t n", t=TT)

            def first_of(vals, top, n, rank):
                eq, best = room(TT * n), room(TT)
                then(tt(eq, vals, top.broadcast_to([P, TT, n]), ALU.is_equal))
                then(tt(eq, eq, bc(rank, 1, TT), ALU.mult))
                then(dve.tensor_reduce(best[:, :, 0], eq, AX, ALU.max))
                then(tt(eq, bc(rank, 1, TT), best.broadcast_to([P, TT, n]), ALU.is_equal))
                return eq

            gmax = room(TT)
            then(dve.tensor_reduce(gmax[:, :, 0], lg[:, :, 0:NG], AX, ALU.max))
            ghot = first_of(lg[:, :, 0:NG], gmax, NG, rank[:, 0:NG])
            el, prod = room(TT * EPG), room(TT * EPG)
            for g in range(NG):
                dst = el if g == 0 else prod
                then(tt(dst, lg[:, :, NG + g * EPG:NG + (g + 1) * EPG],
                        ghot[:, :, g:g + 1].broadcast_to([P, TT, EPG]), ALU.mult))
                if g:
                    then(tt(el, el, prod, ALU.add))
            emax = room(TT)
            then(dve.tensor_reduce(emax[:, :, 0], el, AX, ALU.max))
            sh = rt[:, 0:72].rearrange("p (t c) -> p t c", t=TT)
            then(tt(sh[:, :, 0:NG], lg[:, :, 0:NG], gmax.broadcast_to([P, TT, NG]), ALU.subtract))
            tt(sh[:, :, NG:NG + EPG], el, emax.broadcast_to([P, TT, EPG]), ALU.subtract).then_inc(once("route_shifted_a"), 1)
            dve.wait_ge(once("route_shifted_a"), 1)
            dve.memset(sh[:, :, NG + EPG:nr], 0.0).then_inc(once("route_shifted"), 1)
            lower_tail(MOE0, MOE0 % SLOTS)
            dve.wait_ge(once("route_exp"), 1)
            gs_, es_, w1_, w2_ = room(TT), room(TT), room(TT), room(TT)
            then(dve.tensor_reduce(gs_[:, :, 0], sh[:, :, 0:NG], AX, ALU.add))
            then(dve.tensor_reduce(es_[:, :, 0], sh[:, :, NG:NG + EPG], AX, ALU.add))
            then(dve.reciprocal(gs_[:, :, 0], gs_[:, :, 0]))
            then(dve.reciprocal(es_[:, :, 0], es_[:, :, 0]))
            pe_ = room(TT * EPG)
            then(tt(pe_, sh[:, :, NG:NG + EPG], es_.broadcast_to([P, TT, EPG]), ALU.mult))
            then(dve.tensor_reduce(w1_[:, :, 0], pe_, AX, ALU.max))
            hot1 = first_of(pe_, w1_, EPG, rank)
            rest = room(TT * EPG)
            then(dve.scalar_tensor_tensor(rest, hot1, -2.0, pe_, ALU.mult, ALU.add))
            then(dve.tensor_reduce(w2_[:, :, 0], rest, AX, ALU.max))
            hot2 = first_of(rest, w2_, EPG, rank)
            den = room(TT)
            then(tt(den, w1_, w2_, ALU.add))
            then(dve.reciprocal(den, den))
            then(tt(den, den, gs_, ALU.mult))
            then(tt(w1_, w1_, den, ALU.mult))
            then(tt(w2_, w2_, den, ALU.mult))
            then(tt(hot1, hot1, w1_.broadcast_to([P, TT, EPG]), ALU.mult))
            then(tt(hot2, hot2, w2_.broadcast_to([P, TT, EPG]), ALU.mult))
            then(tt(hot1, hot1, hot2, ALU.add))
            for g in range(NG):
                then(tt(slot_gate[:, :, g * EPG:(g + 1) * EPG], hot1,
                        ghot[:, :, g:g + 1].broadcast_to([P, TT, EPG]), ALU.mult))
            dve.tensor_scalar(chosen, slot_gate[:, :, 0:NE], 0.0, None, ALU.is_gt).then_inc(once("choices_ready"), 1)
            dve.wait_ge(once("choices_ready"), 1)
            lower_tail(MOE0 + 1, (MOE0 + 1) % SLOTS)
            src = wait_filled(dve, l, "count")
            empty(l, "count", dve.tensor_copy(counts, src[:, 0:3 * NE + P]))
            wait_emptied(dve, l, "count")
            wait_emptied(dve, l, "count")
            then(tt(placed, counts[:, 0:TT * NE].rearrange("p (t e) -> p t e", t=TT), chosen, ALU.mult))
            then(dve.tensor_copy(slot_place[:, :, 0:NE], placed))
            then(dve.tensor_scalar(over, counts[:, 2 * NE:3 * NE], float(CAP), None, ALU.is_gt))
            then(dve.tensor_tensor_scan(over_rank, ones_p[:, 0:NE], over, 0.0, ALU.mult, ALU.add))
            for o in range(EXTRA):
                then(dve.scalar_tensor_tensor(over_hot, over_rank, float(o + 1), over, ALU.is_equal, ALU.mult))
                then(tt(picked, placed, bc(over_hot, 1, TT), ALU.mult))
                then(dve.tensor_reduce(slot_place[:, :, NE + o], picked, AX, ALU.add))
                then(tt(picked, slot_gate[:, :, 0:NE], bc(over_hot, 1, TT), ALU.mult))
                then(dve.tensor_reduce(slot_gate[:, :, NE + o], picked, AX, ALU.add))
                then(tt(over_tmp, over_hot, from_one[:, 0:NE], ALU.mult))
                then(dve.tensor_reduce(extra_f[:, o:o + 1], over_tmp, AX, ALU.add))
            for tab in (slot_gate, slot_place):
                then(dve.memset(tab[:, :, WORK:2 * PAIRS], 0.0))
            v_ = slot_place[:, :, NE:WORK]
            then(dve.tensor_scalar(v_, v_, float(-CAP), None, ALU.add))
            then(dve.tensor_scalar(extra_f, extra_f, -1.0, 0.0, ALU.add, ALU.max))
            dve.tensor_copy(extra_ids[:, :], extra_f).then_inc(once("extra_ids_ready"), 1)
            dve.wait_ge(once("extra_ids_ready"), 1)

            def tail_next(s, j):
                lower_tail(moe_piece(s, j) + SLOTS, j % SLOTS)

            def pick_tokens(pair, par):
                at_s = slot_place[:, :, 2 * pair:2 * pair + 2] if isinstance(pair, int) else slot_place[:, :, bass.ds(2 * pair, 2)]
                tt(pick[:, par, :, :].rearrange("p t (b j) -> p t b j", b=2), bc(bc(from_one, 1, 2), 1, TT),
                   bc(at_s, 3, CAP), ALU.is_equal).then_inc(pick_ready, 1)

            def tokens_f32(s, part, f):
                src = moe_filled(dve, 5 - part, s)
                gain = sg_("ffn_g")[:, 2 * f:2 * f + 2]
                tt(xg[:, part, :].rearrange("p (c j) -> p c j", c=2), src[:, :].rearrange("p (c j) -> p c j", c=2),
                   bc(gain, 2, 2 * CAP), ALU.mult).then_inc(bank_emptied[5 - part], 1)
                moe_emptied(dve, use_tokens(s, part))
                dve.sem_inc(xg_f_ready, 1)

            def tokens_lo(s, par, part, f):
                dve.wait_ge(xg_hi_ready, 2 * s + (5 + part))
                cs = slice(f * 512, (f + 1) * 512)
                tt(xg_split[par][1][:, cs], xg[:, part, :], xg_split[par][0][:, cs].bitcast(F32),
                   ALU.subtract).then_inc(xg_ready, 1)

            def output_lo(s):
                for half in range(2):
                    dve.wait_ge(y_hi_ready, 2 * s + 1 + half)
                    cs = slice(half * 512, half * 512 + 512)
                    dve.scalar_tensor_tensor(y_lo[:, cs], bank[6 + half][:, :], gate_of[:, 0:1],
                                             y_hi[:, cs].bitcast(F32), ALU.mult,
                                             ALU.subtract).then_inc(bank_emptied[6 + half], 1)

            def hidden_lo(s):
                dve.wait_ge(hid_hi_ready, s + 1)
                tt(aux_r[:, 512:1024], bank[5][:, :], aux_r[:, 0:512].bitcast(F32),
                   ALU.subtract).then_inc(bank_emptied[5], 1)
                moe_emptied(dve, use_hidden(s))
                dve.sem_inc(hid_ready, 1)

            def step_(s, pair, par, odd, first=False, last=False):
                g = 2 if first else 0
                if not last and not odd:
                    if not first:
                        moe_filled(dve, 6, s - 1)
                    pick_tokens(pair + 1, 1 - par)
                if not first:
                    hidden_lo(s - 1)
                tail_next(s, g)
                tail_next(s, g + 1)
                if not last:
                    tokens_f32(s, 0, 2 * odd)
                if not first:
                    tail_next(s, 2)
                if not last:
                    tokens_lo(s, 1 - par, 0, 2 * odd)
                if not first:
                    tail_next(s, 3)
                    output_lo(s - 1)
                if not last:
                    tokens_f32(s, 1, 2 * odd + 1)
                    tokens_lo(s, 1 - par, 1, 2 * odd + 1)
                moe_emptied(dve, use_gate(s))
                wait_piece(dve, moe_piece(s, 5))
                tt(hid_f, bank[5][:, :], silu_g, ALU.mult).then_inc(bank_emptied[5], 1)
                moe_emptied(dve, use_up(s))
                dve.sem_inc(hid_f_ready, 1)
                tail_next(s, 4)
                if not last:
                    tail_next(s, 5)

            pick_tokens(0, 0)
            lower_tail(MOE0 + 2, (MOE0 + 2) % SLOTS)
            for f in range(4):
                tokens_f32(f // 2 - 2, f % 2, f)
                tokens_lo(f // 2 - 2, 0, f % 2, f)
            step_(0, 0, 0, 0, first=True)
            step_(1, 0, 0, 1)
            with dve.Fori(0, WORK // 4) as r:
                for i in range(4):
                    step_(4 * r + (2 + i), 2 * r + (1 + i // 2), 1 - i // 2, i % 2)
            step_(WORK - 1, PAIRS - 1, (PAIRS - 1) % 2, 0, last=True)
            hidden_lo(WORK - 1)
            output_lo(WORK - 1)
            add_output(l, lambda: dve.wait_ge(once("experts_done"), 1))
            norm(l, 3).then_inc(once("normed_last"), 1)
            dve.wait_ge(once("normed_last"), 1)
            dve.wait_ge(const_in, 16 * 4)
            for t in range(TT):
                tt(nat[:, t, :], nat[:, t, :], row[:, :], ALU.mult).then_inc(once("output_ready"), 1)
                dve.wait_ge(once("output_ready"), t + 1)


def rope_table(pos, scale=1.0):
    half = HD // 2
    inv = (1.0 / (np.float32(ROPE_THETA) ** (np.arange(half, dtype=np.float32) / half))).astype(np.float32)
    ang = (pos.astype(np.float32)[:, None] * inv[None, :]).astype(np.float32)
    return (np.cos(ang) * scale).astype(np.float32), (np.sin(ang) * scale).astype(np.float32)


def shape_constants():
    cc = np.zeros((P, CC_W), np.float32)

    def put(name, value):
        at, n = CC[name]
        cc[:value.shape[0], at:at + n] = value.reshape(value.shape[0], n)

    put("ident", np.eye(P, dtype=np.float32))
    tok = np.arange(SEQ)
    by_tile = lambda v: v.reshape(TT, P, -1).transpose(1, 0, 2).reshape(P, -1)
    cq, sq = rope_table(tok, HD ** -0.5)
    ck, sk = rope_table(tok)
    put("cos_q", by_tile(cq))
    put("sin_q", by_tile(sq))
    put("cos_k", by_tile(ck))
    put("sin_k", by_tile(sk))
    cend = np.arange(NCMP) * CMP_STRIDE + CMP_LEN - 1
    ccos, csin = rope_table(cend)
    pad = lambda v: np.concatenate([np.concatenate([v, np.zeros((CPAD - NCMP, 32), np.float32)])] * 2)
    put("cos_c", pad(ccos))
    put("sin_c", pad(csin))
    i = np.arange(P)
    causal = np.where(i[None, :] <= i[:, None], 0.0, NEG).astype(np.float32)
    put("causal", np.concatenate([np.zeros((P, P), np.float32), causal], axis=1))
    put("tri", (i[:, None] <= i[None, :]).astype(np.float32))
    sees = np.zeros((SEQ, CPAD), bool)
    sees[:, :NCMP] = cend[None, :] <= tok[:, None]
    put("cmp_neg", by_tile(np.where(sees, 0.0, NEG).astype(np.float32)))
    put("cmp_one", by_tile(sees.astype(np.float32)))
    dist = np.zeros((P, 4, 3 * P), np.float32)
    delta = tok[:, None] - tok[None, :]
    rules = [(delta >= 0) & (delta % dil == 0) & (delta <= window) for window, dil in DIL]
    rules.append((delta >= 0) & (delta <= SWA_WIN - 1))
    for n, ok in enumerate(rules):
        d = np.where(ok, -delta, NEG).astype(np.float32)
        dist[:, n, 0:P] = d[0:P, 0:P]
        dist[:, n, P:] = d[P:, :]
    put("dist", dist)
    masks = np.zeros((P, len(LEVELS) + 1, P), np.float32)
    for n, s in enumerate(LEVELS):
        j, q = i[:, None], i[None, :]
        masks[:, n] = (j // (2 * s) == q // (2 * s)) & (j % (2 * s) < s) & (q % (2 * s) >= s)
    masks[:, -1] = np.eye(P, dtype=np.float32)
    return cc, masks.reshape(P, -1)


def kernel(**inputs):
    import numpy as _np
    import concourse.bacc as _bacc
    from concourse.bass_utils import run_bass_kernel_spmd as _run

    v = {k: _np.asarray(a) for k, a in inputs.items()}

    def by_k(w):
        k, n = w.shape
        return w.reshape(k // P, P, n).transpose(1, 0, 2).reshape(P, -1)

    stream = _np.empty((MOE0 + EP * NE, P, PW), _np.float32)
    offs = _np.cumsum((0,) + IN_SIZES)
    (q, kc, vc, ksl, vsl, kwn, vwn, gts, gq, gk, gv, ga, gr, uv) = [
        slice(int(offs[n]), int(offs[n + 1])) for n in range(len(IN_SIZES))]
    lc = _np.zeros((LAYERS, P, LC_W), _np.float32)
    lrow = _np.empty((LAYERS, R_W), _np.float32)

    def ffn_pieces(base, gate, up, down):
        n = gate.shape[1] // CW
        at = base
        for u in range(n + 1):
            todo = []
            if u < n:
                todo.append(by_k(gate[:, u * CW:(u + 1) * CW]))
            if u > 0:
                todo.append(by_k(down[(u - 1) * CW:u * CW, :]))
            if u < n:
                todo.append(by_k(up[:, u * CW:(u + 1) * CW]))
            for piece_ in todo:
                stream[at] = piece_
                at += 1
        return at

    for l in range(LAYERS):
        w = v["w_in"][l]
        order = _np.concatenate([w[:, s] for s in (gq, gk, gv, gr, uv, q, ksl, vsl, kwn, vwn, kc, vc)], axis=1)
        at = l * PIECES1
        for n in range(ZW // CW):
            stream[at + n] = by_k(order[:, n * CW:(n + 1) * CW])
        for first, name in ((P_CMPK, "cmp_w1_k"), (P_CMPV, "cmp_w1_v")):
            for half in range(2):
                stream[at + first + half] = by_k(v[name][l][half * D:(half + 1) * D])
        for n in range(4):
            stream[at + P_OUT + n] = by_k(v["w_out"][l][:, n * CW:(n + 1) * CW])
        ffn_pieces(at + P_FFN, v["w_gate"][l], v["w_up"][l], v["w_down"][l])

        def put(name, value):
            o, n = LC[name]
            lc[l, :, o:o + n] = value.reshape(P, n)

        put("attn_g", v["attn_norm"][l].reshape(KC, P).T)
        put("ffn_g", v["ffn_norm"][l].reshape(KC, P).T)
        put("w_small", by_k(_np.concatenate([w[:, gts], w[:, ga]], axis=1)))
        for n in "kv":
            put(f"pos_{n}", v[f"cmp_pos_{n}"][l].reshape(LP, P).T)
            put(f"w2_{n}", by_k(v[f"cmp_w2_{n}"][l]))
        put("sg_w", v["sg_w"][l].transpose(2, 0, 1))
        put("sg_b", v["sg_b"][l].T)
        put("b_up", v["gla_b_up"][l].reshape(P, 1))
        lrow[l] = _np.concatenate([v["gla_norm"][l], v["sg_ln_g"][l], v["sg_ln_b"][l]])

    w = v["w_in_2"][0]
    for n in range(P_BRD):
        stream[BASE2 + PROJ_AT.get(n, n)] = by_k(w[:, n * CW:(n + 1) * CW])
    for n in range(2):
        stream[BASE2 + P_BRD + n] = by_k(v["w_br_dil_2"][0][:, n * 512:(n + 1) * 512])
    for n in range(4):
        stream[BASE2 + P_BRS + n] = by_k(v["w_br_swa_2"][0][:, n * CW:(n + 1) * CW])
        stream[BASE2 + P_OUT2 + n] = by_k(v["w_out_2"][0][:, n * CW:(n + 1) * CW])
    for e in range(NE):
        at = MOE0 + EP * e
        for n in range(UPE):
            cs = slice(n * CW, (n + 1) * CW)
            stream[at + n] = by_k(v["w_e_gate_2"][0][e][:, cs])
            stream[at + UPE + n] = by_k(v["w_e_up_2"][0][e][:, cs])
            stream[at + 2 * UPE + n] = by_k(v["w_e_down_2"][0][e][cs, :])
    sc = _np.concatenate([v["g_mix_2"][0].reshape(KC, P).T, v["g_ffn_2"][0].reshape(KC, P).T,
                          by_k(_np.concatenate([v["w_group_2"][0], v["w_router_2"][0]], axis=1))], axis=1)
    srow = _np.concatenate([v["b_group_2"][0], v["b_router_2"][0],
                            v["sinks_2"][0]]).reshape(1, S_W)
    cc, masks = shape_constants()
    arrays = {
        "x": _np.ascontiguousarray(v["x"].reshape(SEQ, D)), "stream": stream, "cc": cc, "masks": masks, "lc": lc,
        "lrow": lrow, "w_up": _np.ascontiguousarray(v["gla_w_up"]), "sc": _np.ascontiguousarray(sc), "srow": srow,
        "rows": _np.stack([v["final_norm"], v["g_final_2"]]),
    }
    nc = _bacc.Bacc("TRN2", target_bir_lowering=False, num_devices=1)
    aps = {n: nc.dram_tensor(f"in_{n}", t.shape, mybir.dt.from_np(t.dtype), kind="ExternalInput").ap()
           for n, t in arrays.items()}
    aps["out"] = nc.dram_tensor("out", (SEQ, D), F32, kind="ExternalOutput").ap()
    build_program(nc, aps)
    r = _run(nc, [{f"in_{n}": t for n, t in arrays.items()}], core_ids=[0])
    return r.results[0]["out"].reshape(1, SEQ, D)
```
